# Optimizing a Trainium2 kernel written in Bass

```python
import math
import jax, jax.numpy as jnp
from jax import lax
import numpy as np

D_MODEL = 1024
BATCH = 1
SEQ = 1024
DEPTH = 1
DEC_BATCH = 8
DEC_SEQ = 1
PAST_LEN = 1024
PAGE_SIZE = 128

HEAD_DIM = 64
W_MIX = D_MODEL
W_SB = W_MIX // 2
W_FOX = W_MIX - W_SB
H_SB = W_SB // HEAD_DIM
H_FOX = W_FOX // HEAD_DIM
N_HEADS = H_SB + H_FOX
D_FF = 4 * D_MODEL
N_META = 16
Q_BLOCK = 128
N_IN = 3 * W_SB + 3 * W_FOX + H_FOX
EPS = 1e-6
NEG = -1e30
FORGET_BIAS_INIT = 2.0

kernel_name = "hymba_stickbreaking_fox_decode_step"

def rms_norm(x, g):
    xf = x.astype(jnp.float32)
    y = xf * lax.rsqrt(jnp.mean(xf * xf, axis=-1, keepdims=True) + EPS)
    return (y * g.astype(jnp.float32)).astype(x.dtype)

def project(h, w_in, b_f, q_g, k_g):
    lead = h.shape[:-1]
    p = h @ w_in
    cuts = [int(c) for c in np.cumsum([W_SB, W_SB, W_SB, W_FOX, W_FOX, W_FOX])]
    q_sb, k_sb, v_sb, q_fx, k_fx, v_fx, f = jnp.split(p, cuts, axis=-1)
    heads = lambda t, n: t.reshape(*lead, n, HEAD_DIM)
    q_sb, k_sb, v_sb = heads(q_sb, H_SB), heads(k_sb, H_SB), heads(v_sb, H_SB)
    q_fx = rms_norm(heads(q_fx, H_FOX), q_g)
    k_fx = rms_norm(heads(k_fx, H_FOX), k_g)
    v_fx = heads(v_fx, H_FOX)
    logf = jax.nn.log_sigmoid((f + b_f).astype(jnp.float32))
    return q_sb, k_sb, v_sb, q_fx, k_fx, v_fx, logf

def stick_breaking(q, k, v, qpos, kpos, kvalid):
    z = jnp.einsum('bqhd,bkhd->bhqk', q, k).astype(jnp.float32) / math.sqrt(HEAD_DIM)
    mask = (kpos[None, :] < qpos[:, None]) & kvalid[None, :]
    log_keep = jnp.where(mask, jax.nn.log_sigmoid(-z), 0.0)
    after = lax.cumsum(log_keep, axis=3, reverse=True) - log_keep
    a = jnp.where(mask, jnp.exp(jax.nn.log_sigmoid(z) + after), 0.0)
    return jnp.einsum('bhqk,bkhd->bqhd', a.astype(v.dtype), v)

def forgetting_attn(q, k, v, cq, ck, qpos, kpos, kvalid):
    s = jnp.einsum('bqhd,bkhd->bhqk', q, k).astype(jnp.float32) / math.sqrt(HEAD_DIM)
    s = s + (jnp.swapaxes(cq, 1, 2)[:, :, :, None] - jnp.swapaxes(ck, 1, 2)[:, :, None, :])
    mask = (kpos[None, :] <= qpos[:, None]) & kvalid[None, :]
    p = jax.nn.softmax(jnp.where(mask, s, NEG), axis=-1)
    return jnp.einsum('bhqk,bkhd->bqhd', p.astype(v.dtype), v)

def prompt_mixers(q_sb, k_sb, v_sb, q_fx, k_fx, v_fx, logf):
    pad = (-N_META) % Q_BLOCK
    padf = lambda t: jnp.pad(t, [(0, 0), (pad, 0)] + [(0, 0)] * (t.ndim - 2))
    q_sb, k_sb, v_sb, q_fx, k_fx, v_fx, logf = [padf(t) for t in (q_sb, k_sb, v_sb, q_fx, k_fx, v_fx, logf)]
    b, t_len = q_sb.shape[0], q_sb.shape[1]
    nb = t_len // Q_BLOCK
    kpos = jnp.arange(t_len)
    kvalid = kpos >= pad
    c = jnp.cumsum(logf, axis=1)
    to_blocks = lambda t: jnp.moveaxis(t.reshape(b, nb, Q_BLOCK, *t.shape[2:]), 1, 0)

    def block(args):
        i, qs, qf, cqb = args
        qpos = i * Q_BLOCK + jnp.arange(Q_BLOCK)
        o_sb = stick_breaking(qs, k_sb, v_sb, qpos, kpos, kvalid)
        o_fx = forgetting_attn(qf, k_fx, v_fx, cqb, c, qpos, kpos, kvalid)
        return o_sb, o_fx

    o_sb, o_fx = lax.map(block, (jnp.arange(nb), to_blocks(q_sb), to_blocks(q_fx), to_blocks(c)))
    from_blocks = lambda o: jnp.moveaxis(o, 0, 1).reshape(b, t_len, *o.shape[3:])[:, pad:]
    return from_blocks(o_sb), from_blocks(o_fx)

def gather_pages(pool, page_table):
    g = pool[page_table]
    return g.reshape(g.shape[0], g.shape[1] * g.shape[2], *g.shape[3:])

def merge(o_sb, o_fx, g_sb, g_fx, w_out):
    lead = o_sb.shape[:2]
    o = jnp.concatenate([rms_norm(o_sb.reshape(*lead, W_SB), g_sb),
                         rms_norm(o_fx.reshape(*lead, W_FOX), g_fx)], axis=-1)
    return o @ w_out

def mlp(x, g, w_up, w_down):
    h = rms_norm(x, g)
    return jnp.square(jax.nn.relu(h @ w_up)) @ w_down

def setup_inputs(seed: int = 0) -> dict:
    key = jax.random.key(seed)
    ks = jax.random.split(key, 24)
    n_pages = PAST_LEN // PAGE_SIZE
    n_used = DEC_BATCH * n_pages
    n_pool = n_used + (n_used + 3) // 4
    nrm = lambda k, shape, s=1.0: jax.random.normal(k, shape, jnp.float32) * s
    gain = lambda k, shape: 1.0 + nrm(k, shape, 0.05)
    page_table = jax.random.permutation(ks[5], n_pool)[:n_used].reshape(DEC_BATCH, n_pages).astype(jnp.int32)
    return {
        "x_prompt": nrm(ks[0], (BATCH, SEQ, D_MODEL)),
        "x_sample": nrm(ks[1], (DEC_BATCH, DEC_SEQ, D_MODEL)),
        "cache_k": nrm(ks[2], (DEPTH, n_pool, PAGE_SIZE, N_HEADS, HEAD_DIM)),
        "cache_v": nrm(ks[3], (DEPTH, n_pool, PAGE_SIZE, N_HEADS, HEAD_DIM)),
        "cache_logf": jax.nn.log_sigmoid(FORGET_BIAS_INIT + nrm(ks[4], (DEPTH, n_pool, PAGE_SIZE, H_FOX))),
        "page_table": page_table,
        "meta_tokens": nrm(ks[6], (N_META, D_MODEL)),
        "norm_attn": gain(ks[7], (DEPTH, D_MODEL)),
        "w_in": nrm(ks[8], (DEPTH, D_MODEL, N_IN), D_MODEL ** -0.5),
        "b_forget": FORGET_BIAS_INIT + nrm(ks[9], (DEPTH, H_FOX), 0.5),
        "q_norm": gain(ks[10], (DEPTH, HEAD_DIM)),
        "k_norm": gain(ks[11], (DEPTH, HEAD_DIM)),
        "out_norm_sb": gain(ks[12], (DEPTH, W_SB)),
        "out_norm_fox": gain(ks[13], (DEPTH, W_FOX)),
        "w_out": nrm(ks[14], (DEPTH, W_MIX, D_MODEL), W_MIX ** -0.5),
        "norm_mlp": gain(ks[15], (DEPTH, D_MODEL)),
        "w_up": nrm(ks[16], (DEPTH, D_MODEL, D_FF), D_MODEL ** -0.5),
        "w_down": nrm(ks[17], (DEPTH, D_FF, D_MODEL), D_FF ** -0.5),
    }

def reference(x_prompt, x_sample, cache_k, cache_v, cache_logf, page_table, meta_tokens,
              norm_attn, w_in, b_forget, q_norm, k_norm, out_norm_sb, out_norm_fox,
              w_out, norm_mlp, w_up, w_down):
    b = x_prompt.shape[0]
    xp = jnp.concatenate([jnp.broadcast_to(meta_tokens[None].astype(x_prompt.dtype), (b, N_META, D_MODEL)),
                          x_prompt], axis=1)
    xs = x_sample
    nkp, nvp, nlp, nks, nvs, nls = [], [], [], [], [], []
    for l in range(DEPTH):
        hp = rms_norm(xp, norm_attn[l])
        q_sb, k_sb, v_sb, q_fx, k_fx, v_fx, lf = project(hp, w_in[l], b_forget[l], q_norm[l], k_norm[l])
        o_sb, o_fx = prompt_mixers(q_sb, k_sb, v_sb, q_fx, k_fx, v_fx, lf)
        xp = xp + merge(o_sb, o_fx, out_norm_sb[l], out_norm_fox[l], w_out[l])
        xp = xp + mlp(xp, norm_mlp[l], w_up[l], w_down[l])
        nkp.append(jnp.concatenate([k_sb, k_fx], axis=2))
        nvp.append(jnp.concatenate([v_sb, v_fx], axis=2))
        nlp.append(lf)

        hs = rms_norm(xs, norm_attn[l])
        q_sb, k_sb, v_sb, q_fx, k_fx, v_fx, lf = project(hs, w_in[l], b_forget[l], q_norm[l], k_norm[l])
        k_new = jnp.concatenate([k_sb, k_fx], axis=2)
        v_new = jnp.concatenate([v_sb, v_fx], axis=2)
        k_all = jnp.concatenate([gather_pages(cache_k[l], page_table).astype(k_new.dtype), k_new], axis=1)
        v_all = jnp.concatenate([gather_pages(cache_v[l], page_table).astype(v_new.dtype), v_new], axis=1)
        past = k_all.shape[1] - k_new.shape[1]
        lf_all = jnp.concatenate([gather_pages(cache_logf[l], page_table).astype(jnp.float32), lf], axis=1)
        c = jnp.cumsum(lf_all, axis=1)
        kpos = jnp.arange(k_all.shape[1])
        qpos = past + jnp.arange(k_new.shape[1])
        kvalid = jnp.ones((k_all.shape[1],), dtype=bool)
        o_sb = stick_breaking(q_sb, k_all[:, :, :H_SB], v_all[:, :, :H_SB], qpos, kpos, kvalid)
        o_fx = forgetting_attn(q_fx, k_all[:, :, H_SB:], v_all[:, :, H_SB:], c[:, past:], c,
                               qpos, kpos, kvalid)
        xs = xs + merge(o_sb, o_fx, out_norm_sb[l], out_norm_fox[l], w_out[l])
        xs = xs + mlp(xs, norm_mlp[l], w_up[l], w_down[l])
        nks.append(k_new)
        nvs.append(v_new)
        nls.append(lf)
    y_prompt = xp[:, N_META:]
    y_sample = xs
    return (y_prompt, y_sample, jnp.stack(nkp), jnp.stack(nvp), jnp.stack(nlp),
            jnp.stack(nks), jnp.stack(nvs), jnp.stack(nls))


_drawn_inputs = setup_inputs


def setup_inputs(seed=0):
    import zlib

    import numpy as np

    out = dict(_drawn_inputs(seed))
    spreads = {}
    factors = {}
    for name, (base, spread) in spreads.items():
        noise = np.random.default_rng([zlib.crc32(name.encode()), seed]).standard_normal(out[name].shape)
        drawn = base * np.exp(spread * noise) if base else spread * noise
        out[name] = __import__('jax').numpy.asarray(drawn.astype(out[name].dtype))
    for name, factor in factors.items():
        out[name] = (out[name] * factor).astype(out[name].dtype)
    return out
```

```python
from contextlib import ExitStack

import concourse.bass as bass
import concourse.mybir as mybir
from concourse.alu_op_type import AluOpType as ALU

F32 = mybir.dt.float32
F32R = mybir.dt.float32r
BF16 = mybir.dt.bfloat16
I32 = mybir.dt.int32
ACT = mybir.ActivationFunctionType
AX = mybir.AxisListType

P = 128
D = 1024
KT = D // P
META, SEQ = 16, 1024
TP = META + SEQ
NB = 8
T = TP + NB
HD = 64
H_SB = H_FOX = 8
NH = H_SB + H_FOX
PAIRS = NH // 2
PAGES = 8
EPS = 1e-6
SCALE = HD ** -0.5
NEG = -1e30
FF = 4 * D
BIG = float(2.0 ** 60)
TW = 1152
NBLK = TW // P
CH = [(0, 350), (350, 700), (700, T)]
QC = [(0, 350), (350, 700), (700, TP)]

UNITS = []
for _c, (_a, _b) in enumerate(QC):
    for _j in range((_b - 1) // P, -1, -1):
        for _h in range(2):
            _q0 = max(_a, _j * P)
            UNITS.append((_c, _j, _h, _q0, _b, max(0, min(_b, (_j + 1) * P) - _q0)))
NU = len(UNITS)


SUMS = []
for _s in range(NU + 6):
    if 5 <= _s <= NU + 4 and UNITS[_s - 5][1]:
        SUMS.append(("nrest", _s - 5))
    if 3 <= _s <= NU + 2:
        SUMS.append(("ntri", _s - 3))
N_SUMS = len(SUMS)


def last_of_chunk(u):
    return UNITS[u][1] == 0


def sums_through(u):
    return 1 + max(n for n, (_, v) in enumerate(SUMS) if v == u)


def first_of_chunk(u):
    c = UNITS[u][0]
    return UNITS[u][1] == (QC[c][1] - 1) // P


def finished_before(u):
    return 2 * UNITS[u][0]


class Arena:

    def __init__(self, tensor, size):
        self.t, self.size, self.at = tensor, size, 0

    def take(self, *shape, part=P):
        n = 1
        for s in shape:
            n *= s
        assert self.at + n <= self.size, (self.at, n, self.size)
        ap = self.t[0:part, self.at:self.at + n]
        self.at += n
        if len(shape) == 2:
            ap = ap.rearrange("p (a b) -> p a b", a=shape[0])
        if len(shape) == 3:
            ap = ap.rearrange("p (a b c) -> p a b c", a=shape[0], b=shape[1])
        return ap

    def back(self, at=0):
        self.at = at


def f(ap):
    return ap.bitcast(F32)


def hymba_kernel(nc, x_prompt, x_sample, cache_k, cache_v, cache_logf, page_table, meta_tokens, norm_attn,
                 w_in, b_forget, q_norm, k_norm, out_norm_sb, out_norm_fox, w_out, norm_mlp, w_up, w_down,
                 y_prompt, y_sample, nk_prompt, nv_prompt, nl_prompt, nk_sample, nv_sample, nl_sample):
    ctx = ExitStack()
    with ctx:
        xT_d = nc.dram_tensor("xT_scratch", [KT, P, T], F32).ap()
        oT_d = nc.dram_tensor("oT_scratch", [KT, P, TP], F32).ap()
        qn_d = nc.dram_tensor("q_sample_scratch", [NB, NH * HD], F32).ap()
        s_d = nc.dram_tensor("sample_scores_scratch", [PAIRS // 2, P, NB * PAGES * 4], F32).ap()
        row_d = nc.dram_tensor("row_scratch", [NB, 2 * H_FOX], F32).ap()

        def arena(stack, name, size, dtype=F32):
            return Arena(stack.enter_context(nc.sbuf_tensor(name, [P, size], dtype)), size)

        ps = ctx.enter_context(nc.psum_tensor("ps", [P, 8, 512], F32))
        psf = ps[:, :, :].rearrange("p b n -> p (b n)")
        cf, cr, cb = arena(ctx, "const_f32", 688 + NB * PAGES * (H_FOX + 1)), arena(ctx, "const_f32r", 384, F32R), arena(
            ctx, "const_bf16", 640, BF16)
        sm = cf.take(16)
        c = dict(ident=cf.take(P), ones=cf.take(P), blockones=cf.take(P), lfn=cf.take(NBLK, H_FOX),
                 nck=cf.take(H_FOX, NBLK), o_sample=cf.take(KT, NB),
                 pt=cf.take(NB * PAGES)[0:1, :].bitcast(I32), lfp=cf.take(NB, PAGES, H_FOX),
                 ntri=cr.take(P), nrest=cr.take(P), rones=cr.take(P),
                 identb=cb.take(P), mask_sb=cb.take(P), mask_fox=cb.take(P), mask_q=cb.take(P), mean=cb.take(P),
                 gain=sm[:, 0:KT], eps=sm[:, 8:9], one=sm[:, 9:10], qg=sm[:, 10:11], kg=sm[:, 11:12],
                 bf=sm[0:H_FOX, 12:13],
                 sems=None)
        held = ExitStack()
        used = []

        def hold(s):
            used.append(held.enter_context(s))
            return used[-1]

        def clear_semaphores():
            with nc.Block() as block:
                @block.sync
                def _(sp):
                    for s in used:
                        sp.sem_clear(s)
            used.clear()
            held.pop_all().close()
        c["sems"] = hold
        constants(nc, c)
        with ExitStack() as keep:
            ha = arena(keep, "h_normed", 2 * KT * T, F32R)
            hT = [ha.take(KT, T), ha.take(KT, T)]
            with ExitStack() as st:
                fa = arena(st, "load_f32", KT * T + 4 * D)
                xT = fa.take(KT, T)
                load_and_transpose(nc, fa, ps, c, xT, x_prompt, x_sample, meta_tokens, xT_d)
                fa.back(KT * T)
                rms(nc, "attn", fa, ps, c, xT, [(0, KT, norm_attn[0])], hT)
            with ExitStack() as st:
                fa, ra = arena(st, "gate_f32", 5000), arena(st, "gate_f32r", 2048, F32R)
                forget_gates(nc, fa, ra, ps, c, hT, w_in, b_forget, nl_prompt, nl_sample)
            clear_semaphores()
            with ExitStack() as st:
                fa, ra = arena(st, "pair_f32", 7704), arena(st, "pair_f32r", 15208, F32R)
                head_pairs(nc, fa, ra, ps, psf, c, hT, w_in, q_norm, k_norm, nk_prompt, nv_prompt, nk_sample,
                           nv_sample, qn_d, oT_d, s_d, cache_k, cache_logf, page_table)
        clear_semaphores()
        with ExitStack() as st:
            fa = arena(st, "decode_f32", 50000)
            decode(nc, fa, ps, psf, c, cache_k, cache_v, cache_logf, page_table, qn_d, row_d, s_d, nk_sample,
                   nv_sample, nl_sample)
        with ExitStack() as keep:
            ha = arena(keep, "h_normed2", 2 * KT * T, F32R)
            hT = [ha.take(KT, T), ha.take(KT, T)]
            xa = arena(keep, "x_f32", KT * T)
            xT = xa.take(KT, T)
            with ExitStack() as st:
                fa = arena(st, "o_f32", (KT + 3) * T)
                oT = fa.take(KT, T)
                reload(nc, c, xT, oT, xT_d, oT_d)
                rms(nc, "out", fa, ps, c, oT, [(0, 4, out_norm_sb[0]), (4, 8, out_norm_fox[0])], hT)
            with ExitStack() as st:
                fa, ra = arena(st, "proj_f32", 4 * KT * P), arena(st, "proj_f32r", 4 * KT * P, F32R)
                out_projection(nc, fa, ra, ps, c, hT, xT, w_out)
            with ExitStack() as st:
                fa = arena(st, "norm_f32", 3 * T)
                rms(nc, "mlp", fa, ps, c, xT, [(0, KT, norm_mlp[0])], hT)
            with ExitStack() as st:
                fa = arena(st, "mlp_f32", 4 * KT * P + 2 * T)
                ra = arena(st, "mlp_f32r", 8 * KT * P + 8 * T, F32R)
                mlp(nc, fa, ra, ps, c, hT, xT, w_up, w_down)
            with ExitStack() as st:
                fa = arena(st, "store_f32", 4 * D)
                transpose_and_store(nc, fa, ps, c, xT, y_prompt, y_sample)
        held.close()


def constants(nc, c):
    with ExitStack() as st:
        stage_f = st.enter_context(nc.sbuf_tensor("stage", [P, 5, P], F32))
        built, filled = (c["sems"](nc.semaphore(n)) for n in ("built", "filled"))
        block = st.enter_context(nc.Block())
        jobs = [
            (c["ident"], 0.0, 1, -1, ALU.not_equal, 1.0),
            (stage_f[:, 0, :], -1.0, 1, -1, ALU.is_ge, 0.0),
            (stage_f[:, 1, :], -1.0, -1, 1, ALU.is_gt, 0.0),
            (stage_f[:, 2, :], 0.0, -1, 1, ALU.is_gt, NEG),
            (stage_f[:, 3, :], 0.0, -1, 1, ALU.is_ge, NEG),
            (stage_f[:, 4, :], 0.0, 1, -1, ALU.is_ge, NEG),
        ]

        @block.gpsimd
        def _(pool):
            for ap, start, _, _, _, _ in jobs:
                pool.memset(ap, start).then_inc(filled, 1)
            pool.wait_ge(filled, len(jobs))
            for ap, _, cm, step, op, fill in jobs:
                pool.affine_select(out=ap, in_=ap, compare_op=op, fill=fill, base=0, pattern=[[step, P]],
                                   channel_multiplier=cm).then_inc(built, 1)

        @block.scalar
        def _(act):
            act.preload_act_table_set("natural_log_exp_and_others")

        @block.vector
        def _(dve):
            dve.memset(c["ones"], 1.0)
            dve.memset(c["eps"], EPS)
            dve.memset(c["one"], 1.0)
            dve.memset(f(c["rones"]), 1.0)
            dve.memset(c["mean"], 1.0 / P)
            dve.memset(c["blockones"][0:HD, 0:HD], 1.0)
            dve.memset(c["blockones"][0:HD, HD:P], 0.0)
            dve.memset(c["blockones"][HD:P, 0:HD], 0.0)
            dve.memset(c["blockones"][HD:P, HD:P], 1.0)
            dve.wait_ge(built, len(jobs))
            dve.tensor_copy(c["identb"], c["ident"])
            for n, name in enumerate(("ntri", "nrest", "mask_sb", "mask_fox", "mask_q")):
                dve.tensor_copy(c[name], stage_f[:, n, :])


def product(pe, out, whi, wlo, h, t0, t1, kt):
    for k in range(kt):
        pe.matmul(out, whi[:, k, :], h[0][:, k, t0:t1], start=(k == 0), stop=False)
        pe.matmul(out, whi[:, k, :], h[1][:, k, t0:t1], start=False, stop=False)
        last = pe.matmul(out, wlo[:, k, :], h[0][:, k, t0:t1], start=False, stop=(k == kt - 1))
    return last


def load_and_transpose(nc, fa, ps, c, xT, x_prompt, x_sample, meta_tokens, xT_d):
    nat = fa.take(4, D)
    xp = x_prompt[0]
    with ExitStack() as st:
        sem = lambda n: c["sems"](nc.semaphore(n))
        rows = [sem(f"rows{i}") for i in range(4)]
        turned, moved_a, moved_v, kept = sem("turned"), sem("moved_a"), sem("moved_v"), sem("kept")
        block = st.enter_context(nc.Block())

        @block.sync
        def _(sp):
            for i in range(NBLK):
                if i >= 4:
                    sp.wait_ge(turned, 2 * (i - 3))
                s = nat[:, i % 4, :]
                if i == 0:
                    sp.dma_start(s[0:META, :], meta_tokens).then_inc(rows[0], 16)
                    sp.dma_start(s[META:P, :], xp[0:P - META, :]).then_inc(rows[0], 16)
                elif i < NBLK - 1:
                    sp.dma_start(s, xp[i * P - META:(i + 1) * P - META, :]).then_inc(rows[i % 4], 16)
                else:
                    sp.dma_start(s[0:META, :], xp[SEQ - META:SEQ, :]).then_inc(rows[0], 16)
                    sp.dma_start(s[META:META + NB, :], x_sample[:, 0, :]).then_inc(rows[0], 16)
            sp.wait_ge(moved_a, NBLK)
            sp.wait_ge(moved_v, NBLK)
            sp.dma_start(xT_d.rearrange("k p t -> p k t"), xT).then_inc(kept, 16)
            sp.wait_ge(kept, 16)

        @block.tensor
        def _(pe):
            count = [0] * 4
            for i in range(NBLK):
                count[i % 4] += 32 if i in (0, NBLK - 1) else 16
                pe.wait_ge(rows[i % 4], count[i % 4])
                m = min(P, T - i * P)
                for g in range(2):
                    if i >= 2:
                        pe.wait_ge(moved_v if g else moved_a, i - 1)
                    for k in range(4):
                        last = pe.transpose(ps[:, 2 * (i % 2) + g, k * P:k * P + m],
                                            nat[0:m, i % 4, (4 * g + k) * P:(4 * g + k + 1) * P],
                                            c["ident"][0:m, 0:m])
                    last.then_inc(turned, 1)

        def moves(eng, g, done, copy):
            for i in range(NBLK):
                m = min(P, T - i * P)
                eng.wait_ge(turned, 2 * i + g + 1)
                src = ps[:, 2 * (i % 2) + g, :].rearrange("p (k t) -> p k t", k=4)[:, :, 0:m]
                copy(xT[:, 4 * g:4 * g + 4, i * P:i * P + m], src).then_inc(done, 1)

        @block.scalar
        def _(act):
            moves(act, 0, moved_a, lambda o, i: act.activation(o, i, ACT.Copy))

        @block.vector
        def _(dve):
            moves(dve, 1, moved_v, dve.tensor_copy)


def rms(nc, tag, fa, ps, c, xT, groups, hT):
    at = fa.at
    sq, acc = fa.take(2, T), fa.take(T)
    gain = c["gain"]
    G = len(groups)
    with ExitStack() as st:
        sem = lambda n: c["sems"](nc.semaphore(f"{tag}_{n}"))
        gains, squared, added, summed, root, scaled, hi_done, lo_done = (sem(n) for n in (
            "gains", "squared", "added", "summed", "root", "scaled", "hi", "lo"))
        block = st.enter_context(nc.Block())

        @block.sync
        def _(sp):
            with nc.allow_non_contiguous_dma("gain columns"):
                for a, b, g in groups:
                    sp.dma_start(gain[:, a:b], g.rearrange("(k p) -> p k", p=P)).then_inc(gains, 16)

        @block.scalar
        def _(act):
            n = 0
            for gi, (a, b, _) in enumerate(groups):
                if gi:
                    act.wait_ge(lo_done, a)
                for k in range(a, b):
                    if n >= 2:
                        act.wait_ge(added, n - 1)
                    act.activation(sq[:, n % 2, :], xT[:, k, :], ACT.Square).then_inc(squared, 1)
                    n += 1
                for ci, (t0, t1) in enumerate(CH):
                    act.wait_ge(summed, 3 * gi + ci + 1)
                    act.activation(acc[:, t0:t1], ps[:, ci, 0:t1 - t0], ACT.Ln,
                                   scale=1.0 / ((b - a) * P), bias=c["eps"]).then_inc(root, 1)
                act.wait_ge(root, 4 * gi + 3)
                act.activation(acc, acc, ACT.Exp, scale=-0.5).then_inc(root, 1)
                for k in range(a, b):
                    act.wait_ge(scaled, k + 1)
                    act.activation(hT[0][:, k, :], sq[:, k % 2, :], ACT.Copy).then_inc(hi_done, 1)

        @block.tensor
        def _(pe):
            n = 0
            for gi, (a, b, _) in enumerate(groups):
                n += b - a
                pe.wait_ge(added, n)
                for ci, (t0, t1) in enumerate(CH):
                    if gi:
                        pe.wait_ge(root, 4 * gi)
                    pe.matmul(ps[:, ci, 0:t1 - t0], c["ones"], acc[:, t0:t1], start=True,
                              stop=True).then_inc(summed, 1)

        @block.vector
        def _(dve):
            n = 0
            dve.wait_ge(gains, 16 * G)
            for gi, (a, b, _) in enumerate(groups):
                for k in range(a, b):
                    dve.wait_ge(squared, n + 1)
                    if k == a:
                        dve.tensor_copy(acc, sq[:, n % 2, :]).then_inc(added, 1)
                    else:
                        dve.wait_ge(added, n)
                        dve.tensor_tensor(acc, acc, sq[:, n % 2, :], ALU.add).then_inc(added, 1)
                    n += 1
                dve.wait_ge(root, 4 * gi + 4)
                for k in range(a, b):
                    if k - a >= 2:
                        dve.wait_ge(lo_done, k - 1)
                    dve.scalar_tensor_tensor(sq[:, k % 2, :], xT[:, k, :], gain[:, k:k + 1], acc, ALU.mult,
                                             ALU.mult).then_inc(scaled, 1)
                    if k > a:
                        dve.wait_ge(hi_done, k)
                        dve.tensor_tensor(hT[1][:, k - 1, :], sq[:, (k - 1) % 2, :], f(hT[0][:, k - 1, :]),
                                          ALU.subtract).then_inc(lo_done, 1)
                dve.wait_ge(hi_done, b)
                dve.tensor_tensor(hT[1][:, b - 1, :], sq[:, (b - 1) % 2, :], f(hT[0][:, b - 1, :]),
                                  ALU.subtract).then_inc(lo_done, 1)
                if gi + 1 < G:
                    dve.wait_ge(lo_done, b)
    fa.back(at)


def forget_gates(nc, fa, ra, ps, c, hT, w_in, b_forget, nl_prompt, nl_sample):
    raw = fa.take(KT, P)
    whi, wlo = ra.take(KT, P), ra.take(KT, P)
    fb, e, lf = (fa.take(TW)[0:H_FOX, :] for _ in range(3))
    carry, lfn, nck = fa.take(H_FOX), c["lfn"], c["nck"]
    NF = H_FOX
    with ExitStack() as st:
        sem = lambda n: c["sems"](nc.semaphore(f"fg_{n}"))
        zeroed, loaded, whi_s, wlo_s, proj, biased, expd, capped, logd, gate, turned, nat, sums, stored, scan = (
            sem(n) for n in ("zeroed", "loaded", "whi", "wlo", "proj", "biased", "expd", "capped", "logd",
                             "gate", "turned", "nat", "sums", "stored", "scan"))
        block = st.enter_context(nc.Block())

        @block.sync
        def _(sp):
            sp.wait_ge(zeroed, 2)
            with nc.allow_non_contiguous_dma("eight gate columns"):
                sp.dma_start(raw[:, :, 0:NF], w_in[0][:, 6 * 512:6 * 512 + NF].rearrange(
                    "(k p) n -> p k n", p=P)).then_inc(loaded, 16)
                sp.dma_start(c["bf"], b_forget[0].rearrange("(h a) -> h a", a=1)).then_inc(loaded, 16)
                sp.wait_ge(nat, 1)
                nl = nl_prompt[0, 0]
                sp.dma_start(nl[0:D, :].rearrange("(j p) h -> p j h", p=P), lfn[:, 0:8, :]).then_inc(stored, 16)
                sp.dma_start(nl[D:TP, :], lfn[0:META, 8, :]).then_inc(stored, 16)
                sp.dma_start(nl_sample[0, :, 0, :], lfn[META:META + NB, 8, :]).then_inc(stored, 16)
                sp.wait_ge(stored, 48)

        @block.scalar
        def _(act):
            act.wait_ge(loaded, 32)
            act.activation(whi, raw, ACT.Copy).then_inc(whi_s, 1)
            for ci, (t0, t1) in enumerate(CH):
                act.wait_ge(proj, ci + 1)
                act.activation(fb[:, t0:t1], ps[0:NF, ci, 0:t1 - t0], ACT.Identity,
                               bias=c["bf"]).then_inc(biased, 1)
            act.wait_ge(biased, 3)
            act.activation(e[:, 0:T], fb[:, 0:T], ACT.Exp, scale=-1.0).then_inc(expd, 1)
            act.wait_ge(capped, 1)
            act.activation(e[:, 0:T], e[:, 0:T], ACT.Ln, bias=c["one"][0:NF, :]).then_inc(logd, 1)

        @block.tensor
        def _(pe):
            pe.wait_ge(wlo_s, 1)
            for ci, (t0, t1) in enumerate(CH):
                for k in range(KT):
                    for w, h in ((whi, hT[0]), (whi, hT[1]), (wlo, hT[0])):
                        last = pe.matmul(ps[:, ci, 0:t1 - t0], w[:, k, :], h[:, k, t0:t1],
                                         start=(k == 0 and w is whi and h is hT[0]),
                                         stop=(k == KT - 1 and w is wlo))
                last.then_inc(proj, 1)
            pe.wait_ge(gate, 1)
            for j in range(NBLK):
                last = pe.transpose(ps[:, 3, j * NF:(j + 1) * NF], lf[:, j * P:(j + 1) * P],
                                    c["ident"][0:NF, 0:NF])
            last.then_inc(turned, 1)
            pe.wait_ge(nat, 1)
            flat = lfn.rearrange("p j h -> p (j h)")
            pe.matmul(ps[:, 4, 0:NBLK * NF], f(c["nrest"]), flat, start=True, stop=True)
            pe.matmul(ps[:, 5, 0:NBLK * NF], c["ones"], flat, start=True, stop=True).then_inc(sums, 1)

        @block.vector
        def _(dve):
            dve.memset(raw, 0.0).then_inc(zeroed, 1)
            dve.memset(lf, 0.0).then_inc(zeroed, 1)
            dve.memset(carry, 0.0).then_inc(scan, 1)
            dve.wait_ge(whi_s, 1)
            dve.tensor_tensor(wlo, raw, f(whi), ALU.subtract).then_inc(wlo_s, 1)
            dve.wait_ge(expd, 1)
            dve.tensor_scalar(e[:, 0:T], e[:, 0:T], BIG, None, ALU.min).then_inc(capped, 1)
            dve.wait_ge(logd, 1)
            dve.scalar_tensor_tensor(lf[:, 0:T], e[:, 0:T], -1.0, fb[:, 0:T], ALU.mult,
                                     ALU.min).then_inc(gate, 1)
            dve.wait_ge(turned, 1)
            dve.tensor_copy(lfn, ps[:, 3, 0:NBLK * NF].rearrange("p (j h) -> p j h", h=NF)).then_inc(nat, 1)
            dve.wait_ge(sums, 1)
            dve.wait_ge(nat, 1)
            strict = ps[:, 4, 0:NBLK * NF].rearrange("p (j h) -> p h j", h=NF)
            dve.scalar_tensor_tensor(nck, lfn.rearrange("p j h -> p h j"), -1.0, strict, ALU.mult,
                                     ALU.add).then_inc(scan, 1)
            n = 2
            for j in range(NBLK):
                dve.wait_ge(scan, n)
                dve.tensor_tensor(nck[:, :, j], nck[:, :, j], carry, ALU.subtract).then_inc(scan, 1)
                dve.tensor_tensor(carry, carry, ps[:, 5, j * NF:(j + 1) * NF], ALU.add).then_inc(scan, 1)
                n += 2


def head_pairs(nc, fa, ra, ps, psf, c, hT, w_in, q_norm, k_norm, nk_prompt, nv_prompt, nk_sample, nv_sample,
               qn_d, oT_d, s_d, cache_k, cache_logf, page_table):
    nat = fa.take(2, TW)
    kn, vn = (nat[:, g].rearrange("p (a n) -> p a n", n=P) for g in range(2))
    b = dict(
        qT=fa.take(T), kT=fa.take(TW), vT=fa.take(TW), raw=fa.take(2, KT, P), nat=nat, kn=kn, vn=vn,
        qh=ra.take(2, T), ql=ra.take(2, T), ks=ra.take(2, TW), vs=ra.take(NBLK, 2, P),
        whi=ra.take(2, KT, P), wlo=ra.take(2, KT, P), hi=ra.take(TW), lo=ra.take(TW))
    with nc.Block() as block:
        @block.vector
        def _(dve):
            dve.memset(b["kT"], 0.0)
            dve.memset(b["vT"], 0.0)
    for fox in range(2):
        with ExitStack() as st:
            size_f, size_r = (8472 + 2 * KT * P - 2096, 2800) if fox else (3500, 5600)
            fa = Arena(st.enter_context(nc.sbuf_tensor(f"heads{fox}_f32", [P, size_f], F32)), size_f)
            ra = Arena(st.enter_context(nc.sbuf_tensor(f"heads{fox}_f32r", [P, size_r], F32R)), size_r)
            pair_loop(nc, fox, fa, ra, ps, psf, c, b, hT, w_in, q_norm, k_norm, nk_prompt, nv_prompt,
                      nk_sample, nv_sample, qn_d, oT_d, s_d, cache_k, cache_logf, page_table)


def pair_loop(nc, fox, fa, ra, ps, psf, c, b, hT, w_in, q_norm, k_norm, nk_prompt, nv_prompt, nk_sample,
              nv_sample, qn_d, oT_d, s_d, cache_k, cache_logf, page_table):
    qT, kT, vT, raw, kn, vn, qh, ql, ks, vs, whi, wlo, hi, lo = (b[n] for n in (
        "qT", "kT", "vT", "raw", "kn", "vn", "qh", "ql", "ks", "vs", "whi", "wlo", "hi", "lo"))
    dst = [qT, kT, vT]
    pt, lfp = c["pt"], c["lfp"]
    low_rows = qT
    N_IT = PAIRS // 2
    FL = 4
    RP = 4 if fox else 3
    ph, pl = ra.take(RP, 350), ra.take(RP, 350)
    Z = [0, 1, 2, 7] if fox else [0, 1, 2]
    NZ = len(Z)
    if fox:
        rs = fa.take(T)
        prob = fa.take(5, 350)
        dec_s = fa.take(2 * NB, 16)
        dec_q = b["nat"][:, :, 0:NB * P].rearrange("p g (b n) -> p g b n", b=NB)
        dec_k = [t.rearrange("p k n -> p (k n)").rearrange("p (q g n) -> p q g n", q=PAGES // 2, g=2)
                 for t in (raw[:, 1], fa.take(KT, P))]
        dec_k += [kT[:, 0:KT * P].rearrange("p (q g n) -> p q g n", q=PAGES // 2, g=2),
                  fa.take(KT, P).rearrange("p k n -> p (k n)").rearrange("p (q g n) -> p q g n", q=PAGES // 2, g=2)]
        half = lambda: fa.take(T // 2).bitcast(BF16)
        nckb = [fa.take(TP), fa.take(TP)]
        mrh, mrl = ([t[:, i * TP // 2:(i + 1) * TP // 2].bitcast(BF16) for t in nckb] for i in range(2))
        qb, kb, junk = fa.take(TW // 2).bitcast(BF16), half(), rs.bitcast(BF16)
        nckp, mx = fa.take(2, NBLK), fa.take(2, NBLK)
        nmh, nml = fa.take(NBLK).bitcast(BF16), fa.take(NBLK).bitcast(BF16)
        zc, ee, sph, spl = None, None, None, None
    else:
        zc, ee, sph, spl = fa.take(6, 350), fa.take(4, 350), ra.take(5, 350), ra.take(5, 350)
    tag = "fx" if fox else "sb"
    with ExitStack() as st:
        sem = lambda n: c["sems"](nc.semaphore(f"{tag}_{n}"))
        w_loaded = [sem("w_loaded0"), sem("w_loaded1")]
        w_hi, w_lo, proj, evac, carry = sem("w_hi"), sem("w_lo"), sem("proj"), sem("evac"), sem("carry")
        split_hi, split_lo, dup = sem("split_hi"), sem("split_lo"), sem("dup")
        k_turned, v_turned, k_nat, v_nat, v_hi, v_lo, stored, o_stored = (sem(n) for n in (
            "k_turned", "v_turned", "k_nat", "v_nat", "v_hi", "v_lo", "stored", "o_stored"))
        fin_moved, fin = sem("fin_moved"), sem("fin")
        pair_free, v_free = sem("pair_free"), sem("v_free")
        z_done, p_done, ph_done, pl_done, pv_done = (sem(n) for n in (
            "z_done", "p_done", "ph_done", "pl_done", "pv_done"))
        if fox:
            g_loaded, squared, ssum, root, normed, fin_part, den_log, den_inv = (sem(n) for n in (
                "g_loaded", "squared", "ssum", "root", "normed", "fin_part", "den_log", "den_inv"))
            dq_in, dk_in, dk_mult, dk_half, dk_free, ds_stored, dstep = (sem(n) for n in (
                "dq_in", "dk_in", "dk_mult", "dk_half", "dk_free", "ds_stored", "dstep"))
            dk_in = [dk_in] + [sem(f"dk_in{i}") for i in range(1, 4)]
            qkb, nck_ps, nck_sb, s_done, mxd, nm_h, nm_l, mr_ps, mr_h, mr_l, setup, stepped = (sem(n) for n in (
                "qkb", "nck_ps", "nck_sb", "s_done", "mxd", "nm_h", "nm_l", "mr_ps", "mr_h", "mr_l", "setup", "stepped"))
        else:
            pt_in, lf_in, stepped = sem("pt_in"), sem("lf_in"), sem("stepped")
            e_done, z_kept, e_cap, l_done, sp_done, sph_done, spl_done, tri, x_done = (sem(n) for n in (
                "e_done", "z_kept", "e_cap", "l_done", "sp_done", "sph_done", "spl_done", "tri", "x_done"))
        block = st.enter_context(nc.Block())

        @block.sync
        def _(sp):
            if fox:
                with nc.allow_non_contiguous_dma("gain columns"):
                    for g, src in ((c["qg"], q_norm), (c["kg"], k_norm)):
                        for h in range(2):
                            sp.dma_start(g[h * HD:(h + 1) * HD, :], src[0].rearrange("(d a) -> d a", a=1)
                                         ).then_inc(g_loaded, 16)
            else:
                sp.dma_start(pt, page_table.rearrange("(a b) n -> a (b n)", a=1)).then_inc(pt_in, 16)
                sp.wait_ge(pt_in, 16)
            sp.sem_inc(pair_free, 1)
            sp.sem_inc(v_free, 1)

            def load_weights(it, t):
                src = w_in[0][:, bass.ds(it * P + (fox * 3 + t) * 512, P)]
                sp.dma_start(raw[:, t % 2, :, :], src.rearrange("(k p) n -> p k n", p=P)
                             ).then_inc(w_loaded[t % 2], 16)

            load_weights(0, 0)
            load_weights(0, 1)
            with sp.Fori(0, N_IT) as it:
                sp.wait_ge(w_lo, it * 3 + 1)
                sp.sem_inc(carry, 1)
                load_weights(it, 2)
                sp.wait_ge(split_lo, it * 2 + 1)
                for src, to in ((hi, qh), (lo, ql)):
                    for h in range(2):
                        for half_ in range(2):
                            sp.dma_start(f(to[half_ * HD:(half_ + 1) * HD, h, :]),
                                         f(src[h * HD:(h + 1) * HD, 0:T])).then_inc(dup, 16)
                sp.wait_ge(split_lo, it * 2 + 2)
                for h in range(2):
                    for n, src in enumerate((hi, lo)):
                        sp.dma_start(f(ks[n * HD:(n + 1) * HD, h, :]), f(src[h * HD:(h + 1) * HD, :])
                                     ).then_inc(dup, 16)
                col = bass.ds(it * P + fox * 512, P)
                for nat, done, per, prompt, sample in ((kn, k_nat, 3, nk_prompt, nk_sample),
                                                       (vn, v_nat, 3, nv_prompt, nv_sample)):
                    sp.wait_ge(done, it * per + per)
                    sp.sem_inc(carry, 1)
                    rows = prompt[0, 0].rearrange("t h d -> t (h d)")[:, col]
                    sp.dma_start(rows[0:D, :].rearrange("(j p) n -> p j n", p=P), nat[:, 0:8, :]
                                 ).then_inc(stored, 16)
                    sp.dma_start(rows[D:TP, :], nat[0:META, 8, :]).then_inc(stored, 16)
                    sp.dma_start(sample[0, :, 0].rearrange("b h d -> b (h d)")[:, col],
                                 nat[META:META + NB, 8, :]).then_inc(stored, 16)
                with nc.allow_non_contiguous_dma("eight columns"):
                    sp.dma_start(qn_d[:, col].rearrange("b n -> n b"), qT[:, TP:T]).then_inc(stored, 16)
                sp.wait_ge(w_lo, it * 3 + 3)
                sp.sem_inc(carry, 1)
                load_weights(it + 1, 0)
                if not fox:
                    load_weights(it + 1, 1)
                if fox:
                    sp.wait_ge(v_lo, it * 3 + 3)
                    sp.sem_inc(carry, 1)
                    sp.wait_ge(stored, it * 112 + 112)
                    sp.sem_inc(carry, 1)
                    for g in range(2):
                        sp.dma_start(dec_q[:, g], qn_d[:, bass.ds(it * P + g * 512, P)].partition_broadcast(P)
                                     ).then_inc(dq_in, 16)
                    sp.wait_ge(qkb, it * 2 + 2)
                    sp.sem_inc(carry, 1)
                    with sp.Fori(0, NB // 2) as b_:
                        for m in range(2 * PAGES):
                            page = sp.value_load(pt[0:1, bass.ds(b_ * (2 * PAGES) + m, 1)], min_val=0,
                                                 max_val=cache_k.shape[1] - 1)
                            slot = m // (PAGES // 2)
                            if m % (PAGES // 2) == 0:
                                sp.wait_ge(dk_free, it * (2 * NB) + b_ * 4 + slot + 1)
                                sp.sem_inc(carry, 1)
                            src = cache_k[0, bass.ds(page, 1)].rearrange("a r h d -> r (a h d)").rearrange(
                                "r (g n) -> r g n", g=2)[:, :, bass.ds(it * P, P)]
                            sp.dma_start(dec_k[slot][:, m % (PAGES // 2)], src).then_inc(dk_in[slot], 16)
                    sp.wait_ge(dk_free, it * (2 * NB) + 2 * NB + 4)
                    sp.sem_inc(carry, 1)
                    sp.dma_start(s_d[bass.ds(it, 1)].rearrange("a p n -> p (a n)"),
                                 dec_s.rearrange("p b n -> p (b n)")).then_inc(ds_stored, 16)
                if not fox:
                    for m in range(2 * PAGES):
                        page = sp.value_load(pt[0:1, bass.ds(it * (2 * PAGES) + m, 1)], min_val=0,
                                             max_val=cache_k.shape[1] - 1)
                        sp.dma_start(lfp[:, bass.ds(it * 2 + m // PAGES, 1), m % PAGES, :].rearrange(
                            "p a h -> p (a h)"), cache_logf[0, bass.ds(page, 1)].rearrange("a r h -> r (a h)")
                        ).then_inc(lf_in, 16)
                    sp.wait_ge(lf_in, it * (32 * PAGES) + 32 * PAGES)
                    sp.sem_inc(stepped, 1)
                if fox:
                    load_weights(it + 1, 1)
                sp.wait_ge(fin, it * 6 + 6)
                sp.sem_inc(carry, 1)
                if not fox:
                    sp.wait_ge(stored, it * 112 + 112)
                sp.sem_inc(pair_free, 1)
                sp.dma_start(oT_d[bass.ds(it + fox * N_IT, 1)].rearrange("a p t -> p (a t)"), vT[:, 0:TP]
                             ).then_inc(o_stored, 16)
                if fox:
                    sp.wait_ge(ds_stored, it * 16 + 16)
                    sp.sem_inc(carry, 1)
                sp.wait_ge(o_stored, it * 16 + 16)
                sp.sem_inc(v_free, 1)
            for t in range(2):
                sp.wait_ge(w_loaded[t], 16 * (N_IT * (2 - t) + 1))

        @block.scalar
        def _(act):
            def weights_hi(it, t):
                act.wait_ge(w_loaded[t % 2], (it * 32 + 16 + (16 if t == 2 else 0)) if t % 2 == 0
                            else it * 16 + 16)
                if t == 2:
                    act.wait_ge(proj, it * 9 + 3)
                act.activation(whi[:, t % 2], raw[:, t % 2], ACT.Copy).then_inc(w_hi, 1)

            weights_hi(0, 0)
            with act.Fori(0, N_IT) as it:
                def take(t, chunks=(0, 1, 2)):
                    if t == 2 and chunks[0] == 0:
                        act.wait_ge(v_free, it + 1)
                    for ci in chunks:
                        t0, t1 = CH[ci]
                        act.wait_ge(proj, it * 9 + 3 * t + ci + 1)
                        act.activation(dst[t][:, t0:t1], ps[:, ci, 0:t1 - t0], ACT.Copy,
                                       scale=SCALE if (t == 0 and not fox) else 1.0).then_inc(evac, 1)

                def square(t):
                    act.wait_ge(evac, it * 9 + 3 * t + 3)
                    if t:
                        act.wait_ge(normed, it * 2 + 1)
                    act.activation(rs, dst[t][:, 0:T], ACT.Square).then_inc(squared, 1)

                def norm(t):
                    for ci, (t0, t1) in enumerate(CH):
                        act.wait_ge(ssum, it * 6 + 3 * t + 3)
                        act.activation(rs[:, t0:t1], ps[:, 3 + ci, 0:t1 - t0], ACT.Ln, scale=1.0 / HD,
                                       bias=c["eps"]).then_inc(root, 1)
                    act.wait_ge(root, it * 8 + 4 * t + 3)
                    act.activation(rs, rs, ACT.Exp, scale=-0.5).then_inc(root, 1)

                def split(t):
                    if fox:
                        act.wait_ge(normed, it * 2 + t + 1)
                    else:
                        act.wait_ge(evac, it * 9 + 3 * t + 3)
                    if t:
                        act.wait_ge(dup, it * 192 + 128)
                    w = T if t == 0 else TW
                    act.activation(hi[:, 0:w], dst[t][:, 0:w], ACT.Copy).then_inc(split_hi, 1)

                def k_rows():
                    for g in range(3):
                        act.wait_ge(k_turned, it * 3 + g + 1)
                        w = 4 if g < 2 else 1
                        act.activation(kn[:, 4 * g:4 * g + w, :], ps[:, 3 + g, 0:w * P].rearrange(
                            "p (j n) -> p j n", n=P), ACT.Copy).then_inc(k_nat, 1)

                weights_hi(it, 1)
                act.wait_ge(pair_free, it + 1)
                take(0)
                weights_hi(it, 2)
                if fox:
                    square(0)
                    take(1, (0,))
                    norm(0)
                    take(1, (1,))
                    split(0)
                    take(1, (2,))
                    square(1)
                    take(2, (0,))
                    norm(1)
                    take(2, (1,))
                    split(1)
                    take(2, (2,))
                    k_rows()
                else:
                    split(0)
                    take(1)
                    split(1)
                    take(2, (0,))
                    k_rows()
                    take(2, (1, 2))
                for g in range(3):
                    w = 4 if g < 2 else 1
                    act.wait_ge(v_nat, it * 3 + g + 1)
                    act.activation(vs[:, 4 * g:4 * g + w, :, 0:HD],
                                   vn[:, 4 * g:4 * g + w, :].rearrange("p j (h d) -> p j h d", h=2),
                                   ACT.Copy).then_inc(v_hi, 1)

                def finish(u):
                    act.wait_ge(pv_done, it * NU + u + 1)
                    cc, _, h, _, _, _ = UNITS[u]
                    n = finished_before(u) + h
                    if n:
                        act.wait_ge(fin, it * 6 + n)
                    w = QC[cc][1] - QC[cc][0]
                    act.activation(low_rows[0:HD, 0:w], ps[HD:P, 5 + h, 0:w], ACT.Copy).then_inc(fin_moved, 1)
                    if fox:
                        inv = low_rows[0:HD, 400:400 + w]
                        act.activation(inv, ps[0:HD, 3 + h, 0:w], ACT.Ln).then_inc(den_log, 1)
                        act.wait_ge(den_log, it * 6 + finished_before(u) + h + 1)
                        act.activation(inv, inv, ACT.Exp, scale=-1.0).then_inc(den_inv, 1)

                if fox:
                    for h in range(2):
                        base = 5 * 512 * (1 - h)
                        act.wait_ge(nck_ps, it * 2 + h + 1)
                        act.activation(nckb[h], psf[:, base:base + TP], ACT.Copy).then_inc(nck_sb, 1)
                    act.wait_ge(mxd, it * 18 + 18)
                    act.activation(nmh[:, 0:18], mx.rearrange("p h j -> p (h j)"), ACT.Copy,
                                   scale=-1.0).then_inc(nm_h, 1)
                    for h in range(2):
                        act.wait_ge(mr_ps, it * 2 + h + 1)
                        act.activation(mrh[h][:, 0:TP], psf[:, 5 * 512 * h:5 * 512 * h + TP],
                                       ACT.Copy).then_inc(mr_h, 1)
                    for s in range(NU + FL):
                        if s < NU:
                            cc, j, h, q0, q1, _ = UNITS[s]
                            n = q1 - q0
                            act.wait_ge(z_done, it * NU + s + 1)
                            if s >= 5:
                                act.wait_ge(pl_done, it * NU + s - 4)
                            act.activation(prob[:, s % 5, 0:n], ps[:, Z[s % NZ], 0:n], ACT.Exp,
                                           bias=nckp[:, h, j:j + 1]).then_inc(p_done, 1)
                        if s >= FL and last_of_chunk(s - FL):
                            finish(s - FL)
                else:
                    for s in range(NU + 7):
                        if s < NU:
                            _, _, _, q0, q1, _ = UNITS[s]
                            n = q1 - q0
                            act.wait_ge(z_kept, it * NU + s + 1)
                            if s >= 4:
                                act.wait_ge(spl_done, it * NU + s - 3)
                            act.activation(ee[:, s % 4, 0:n], zc[:, s % 6, 0:n], ACT.Exp).then_inc(e_done, 1)
                        if 1 <= s <= NU:
                            u = s - 1
                            n = UNITS[u][4] - UNITS[u][3]
                            act.wait_ge(e_cap, it * NU + u + 1)
                            act.activation(ee[:, u % 4, 0:n], ee[:, u % 4, 0:n], ACT.Ln,
                                           bias=c["one"]).then_inc(l_done, 1)
                        if 2 <= s <= NU + 1:
                            u = s - 2
                            n = UNITS[u][4] - UNITS[u][3]
                            act.wait_ge(sp_done, it * NU + u + 1)
                            if u >= 5:
                                act.wait_ge(tri, it * N_SUMS + sums_through(u - 5))
                            act.activation(sph[:, u % 5, 0:n], ee[:, u % 4, 0:n], ACT.Copy).then_inc(sph_done, 1)
                        if 4 <= s <= NU + 3:
                            u = s - 4
                            n = UNITS[u][4] - UNITS[u][3]
                            act.wait_ge(x_done, it * NU + u + 1)
                            act.activation(zc[:, u % 6, 0:n], zc[:, u % 6, 0:n], ACT.Exp).then_inc(p_done, 1)
                        if s >= 7 and last_of_chunk(s - 7):
                            finish(s - 7)
                weights_hi(it + 1, 0)

        @block.vector
        def _(dve):
            if fox:
                dve.memset(qb[:, T:TW], 0.0).then_inc(setup, 1)
                dve.wait_ge(g_loaded, 64)
                dve.tensor_scalar(c["qg"], c["qg"], SCALE, None, ALU.mult).then_inc(setup, 1)
                dve.wait_ge(setup, 2)
            def weights_lo(it, t):
                dve.wait_ge(w_hi, it * 3 + t + 1)
                dve.tensor_tensor(wlo[:, t % 2], raw[:, t % 2], f(whi[:, t % 2]), ALU.subtract
                                  ).then_inc(w_lo, 1)

            weights_lo(0, 0)
            with dve.Fori(0, N_IT) as it:

                def norm(t):
                    dve.wait_ge(root, it * 8 + 4 * t + 4)
                    dve.scalar_tensor_tensor(dst[t][:, 0:T], dst[t][:, 0:T], c["kg" if t else "qg"], rs,
                                             ALU.mult, ALU.mult).then_inc(normed, 1)

                def split(t):
                    dve.wait_ge(split_hi, it * 2 + t + 1)
                    w = T if t == 0 else TW
                    dve.tensor_tensor(lo[:, 0:w], dst[t][:, 0:w], f(hi[:, 0:w]), ALU.subtract
                                      ).then_inc(split_lo, 1)

                weights_lo(it, 1)
                weights_lo(it, 2)
                if fox:
                    dve.tensor_copy(nckp, c["nck"][:, bass.ds(it * 2, 2), :]).then_inc(setup, 1)
                    norm(0)
                split(0)
                if fox:
                    norm(1)
                split(1)
                if fox:
                    dve.wait_ge(normed, it * 2 + 2)
                    dve.tensor_copy(qb[:, 0:T], qT).then_inc(qkb, 1)
                    dve.tensor_copy(kb[:, 0:T], kT[:, 0:T]).then_inc(qkb, 1)
                for g in range(3):
                    w = 4 if g < 2 else 1
                    dve.wait_ge(v_turned, it * 3 + g + 1)
                    dve.tensor_copy(vn[:, 4 * g:4 * g + w, :], ps[:, 5 + (g + 1) % 3, (P if g == 2 else 0):
                                                                  (P if g == 2 else 0) + w * P].rearrange(
                        "p (j n) -> p j n", n=P)).then_inc(v_nat, 1)
                for g in range(3):
                    w = 4 if g < 2 else 1
                    dve.wait_ge(v_hi, it * 3 + g + 1)
                    dve.tensor_tensor(vs[:, 4 * g:4 * g + w, :, HD:P],
                                      vn[:, 4 * g:4 * g + w, :].rearrange("p j (h d) -> p j h d", h=2),
                                      f(vs[:, 4 * g:4 * g + w, :, 0:HD]), ALU.subtract).then_inc(v_lo, 1)

                def split_p(u, src):
                    n = UNITS[u][4] - UNITS[u][3]
                    dve.wait_ge(p_done, it * NU + u + 1)
                    if u >= RP:
                        dve.wait_ge(pv_done, it * NU + u - RP + 1)
                    dve.tensor_copy(ph[:, u % RP, 0:n], src).then_inc(ph_done, 1)
                    dve.wait_ge(ph_done, it * NU + u + 1)
                    dve.tensor_tensor(pl[:, u % RP, 0:n], src, f(ph[:, u % RP, 0:n]), ALU.subtract
                                      ).then_inc(pl_done, 1)

                def finish(u):
                    cc, _, h, _, _, _ = UNITS[u]
                    n = finished_before(u) + h
                    q0, q1 = QC[cc]
                    o = vT[h * HD:(h + 1) * HD, q0:q1]
                    dve.wait_ge(fin_moved, it * 6 + n + 1)
                    if not fox:
                        dve.tensor_tensor(o, ps[0:HD, 5 + h, 0:q1 - q0], low_rows[0:HD, 0:q1 - q0], ALU.add
                                          ).then_inc(fin, 1)
                    else:
                        t0, t1 = low_rows[0:HD, 0:q1 - q0], low_rows[0:HD, 400:400 + q1 - q0]
                        dve.tensor_tensor(t0, ps[0:HD, 5 + h, 0:q1 - q0], t0, ALU.add).then_inc(fin_part, 1)
                        dve.wait_ge(den_inv, it * 6 + n + 1)
                        dve.wait_ge(fin_part, it * 6 + n + 1)
                        dve.tensor_tensor(o, t0, t1, ALU.mult).then_inc(fin, 1)

                def sample_scores(k):
                    dve.wait_ge(dk_half, it * (2 * NB) + k + 1)
                    if k == 0:
                        dve.wait_ge(v_free, it + 1)
                    x = dec_k[k % 4].rearrange("p q g (h d) -> p (q g h) d", h=2)[:, :, 0:HD // 2]
                    dve.tensor_reduce(dec_s[:, k, :], x, AX.X, ALU.add).then_inc(dk_free, 1)

                if fox:
                    for n in range(18):
                        if n in (9, 12, 15):
                            sample_scores(n // 3 - 3)
                        h, i = divmod(n, 9)
                        m = min(P, TP - i * P)
                        w = i * P + m
                        base = 5 * 512 * (n % 2)
                        dve.wait_ge(s_done, it * 18 + n + 1)
                        if n < 2:
                            dve.wait_ge(nck_sb, it * 2 + 2)
                        if n:
                            dve.wait_ge(mxd, it * 18 + n)
                        dve.sem_inc(stepped, 1)
                        dve.tensor_tensor_reduce(out=junk[:, 0:w], in0=psf[:, base:base + w],
                                                 in1=nckb[h][:, 0:w], scale=1.0, scalar=NEG, op0=ALU.add,
                                                 op1=ALU.max, accum_out=mx[:, h, i:i + 1]).then_inc(mxd, 1)
                    dve.wait_ge(nm_h, it + 1)
                    dve.wait_ge(mxd, it * 18 + 18)
                    dve.scalar_tensor_tensor(nml[:, 0:18], mx.rearrange("p h j -> p (h j)"), -1.0,
                                             nmh[:, 0:18], ALU.mult, ALU.subtract).then_inc(nm_l, 1)
                    for h in range(2):
                        dve.wait_ge(mr_h, it * 2 + h + 1)
                        dve.tensor_tensor(mrl[h][:, 0:TP], psf[:, 5 * 512 * h:5 * 512 * h + TP],
                                          mrh[h][:, 0:TP], ALU.subtract).then_inc(mr_l, 1)
                    sample_scores(3)
                    for u in range(NU + FL):
                        if u < NU and u % 3 == 2:
                            sample_scores(4 + u // 3)
                        if u < NU:
                            split_p(u, prob[:, u % 5, 0:UNITS[u][4] - UNITS[u][3]])
                        if u >= FL and last_of_chunk(u - FL):
                            finish(u - FL)
                else:
                    for s in range(NU + 7):
                        if s < NU:
                            n = UNITS[s][4] - UNITS[s][3]
                            dve.wait_ge(z_done, it * NU + s + 1)
                            if s >= 6:
                                dve.wait_ge(pl_done, it * NU + s - 5)
                            dve.tensor_copy(zc[:, s % 6, 0:n], ps[:, s % 3, 0:n]).then_inc(z_kept, 1)
                        if 5 <= s <= NU + 4:
                            u = s - 5
                            split_p(u, zc[:, u % 6, 0:UNITS[u][4] - UNITS[u][3]])
                        if s < NU:
                            dve.wait_ge(e_done, it * NU + s + 1)
                            dve.tensor_scalar(ee[:, s % 4, 0:n], ee[:, s % 4, 0:n], BIG, None, ALU.min
                                              ).then_inc(e_cap, 1)
                        if 1 <= s <= NU:
                            u = s - 1
                            n = UNITS[u][4] - UNITS[u][3]
                            dve.wait_ge(l_done, it * NU + u + 1)
                            dve.wait_ge(z_kept, it * NU + u + 1)
                            dve.tensor_tensor(ee[:, u % 4, 0:n], ee[:, u % 4, 0:n], zc[:, u % 6, 0:n],
                                              ALU.max).then_inc(sp_done, 1)
                        if 3 <= s <= NU + 2:
                            u = s - 3
                            cc, _, h, q0, q1, _ = UNITS[u]
                            n, off = q1 - q0, q0 - QC[cc][0]
                            dve.wait_ge(tri, it * N_SUMS + SUMS.index(("ntri", u)) + 1)
                            dve.tensor_tensor(zc[:, u % 6, 0:n], zc[:, u % 6, 0:n],
                                              ps[:, 3 + h, off:off + n], ALU.add).then_inc(x_done, 1)
                        if s >= 7 and last_of_chunk(s - 7):
                            finish(s - 7)
                weights_lo(it + 1, 0)

        if not fox:
            @block.gpsimd
            def _(pool):
                with pool.Fori(0, N_IT) as it:
                    for u in range(NU):
                        n = UNITS[u][4] - UNITS[u][3]
                        pool.wait_ge(sph_done, it * NU + u + 1)
                        pool.tensor_tensor(spl[:, u % 5, 0:n], ee[:, u % 4, 0:n], f(sph[:, u % 5, 0:n]),
                                           ALU.subtract).then_inc(spl_done, 1)

        else:
            @block.gpsimd
            def _(pool):
                pool.sem_inc(dk_free, 4)
                with pool.Fori(0, N_IT) as it:
                    pool.wait_ge(dq_in, it * 32 + 32)
                    pool.sem_inc(dstep, 1)
                    with pool.Fori(0, NB // 2) as b_:
                        for slot in range(4):
                            k = dec_k[slot]
                            pool.wait_ge(dk_in[slot], it * (64 * NB // 2) + b_ * 64 + 64)
                            pool.sem_inc(dstep, 1)
                            q = dec_q[:, :, bass.ds(b_ * 2 + slot // 2, 1), :].rearrange("p g a n -> p a g n")
                            pool.tensor_tensor(k, k, q.broadcast_to([P, PAGES // 2, 2, P]), ALU.mult
                                               ).then_inc(dk_mult, 1)
                            pool.wait_ge(dk_mult, it * (2 * NB) + b_ * 4 + slot + 1)
                            x = k.rearrange("p q g (h d) -> p (q g h) d", h=2)
                            pool.tensor_tensor(x[:, :, 0:HD // 2], x[:, :, 0:HD // 2], x[:, :, HD // 2:HD],
                                               ALU.add).then_inc(dk_half, 1)
                    pool.sem_inc(dstep, 1)

        @block.tensor
        def _(pe):
            with pe.Fori(0, N_IT) as it:
                def turn_k():
                    if fox:
                        pe.wait_ge(normed, it * 2 + 2)
                    else:
                        pe.wait_ge(evac, it * 9 + 6)
                    for g in range(3):
                        for j in range(4 * g, min(NBLK, 4 * g + 4)):
                            last = pe.transpose(ps[:, 3 + g, (j % 4) * P:(j % 4 + 1) * P],
                                                kT[:, j * P:(j + 1) * P], c["ident"])
                        last.then_inc(k_turned, 1)

                for t in range(3):
                    pe.wait_ge(w_lo, it * 3 + t + 1)
                    for ci, (t0, t1) in enumerate(CH):
                        if t:
                            pe.wait_ge(evac, it * 9 + 3 * (t - 1) + ci + 1)
                        product(pe, ps[:, ci, 0:t1 - t0], whi[:, t % 2], wlo[:, t % 2], hT, t0, t1, KT
                                ).then_inc(proj, 1)
                        if fox and t and ci == 0:
                            for cs, (s0, s1) in enumerate(CH):
                                pe.wait_ge(squared, it * 2 + t)
                                pe.matmul(ps[:, 3 + cs, 0:s1 - s0], c["blockones"], rs[:, s0:s1], start=True,
                                          stop=True).then_inc(ssum, 1)
                        if not fox and t == 2 and ci == 0:
                            turn_k()
                for g in range(3):
                    if g == 1 and fox:
                        turn_k()
                    if g == 2:
                        pe.wait_ge(k_nat, it * 3 + 3)
                    pe.wait_ge(evac, it * 9 + (9 if g else 8))
                    for j in range(4 * g, min(NBLK, 4 * g + 4)):
                        n0 = P if g == 2 else (j % 4) * P
                        last = pe.transpose(ps[:, 5 + (g + 1) % 3, n0:n0 + P], vT[:, j * P:(j + 1) * P],
                                            c["ident"])
                    last.then_inc(v_turned, 1)
                if fox:
                    pe.wait_ge(v_nat, it * 3 + 3)

                def scores(s, extra):
                    cc, j, h, q0, q1, mask = UNITS[s]
                    n = q1 - q0
                    z = ps[:, Z[s % NZ], 0:n]
                    key = ks[:, h, j * P:(j + 1) * P]
                    pe.matmul(z, key, qh[:, h, q0:q1], start=True, stop=False)
                    if mask:
                        off = q0 - j * P
                        pe.matmul(z[:, 0:mask], c["identb"],
                                  c["mask_fox" if fox else "mask_sb"][:, off:off + mask], start=False,
                                  stop=False, skip_group_check=True)
                    if extra:
                        pe.matmul(z, c["mean"], mrh[h][:, q0:q1], start=False, stop=False)
                        pe.matmul(z, c["mean"], mrl[h][:, q0:q1], start=False, stop=False)
                    last = pe.matmul(z, key, ql[:, h, q0:q1], start=False, stop=True)
                    last.then_inc(z_done, 1)

                def values(u):
                    cc, j, h, q0, q1, _ = UNITS[u]
                    n, off = q1 - q0, q0 - QC[cc][0]
                    first, end = first_of_chunk(u), last_of_chunk(u)
                    if first and cc:
                        done = it * 6 + 2 * (cc - 1) + h + 1
                        if fox:
                            pe.wait_ge(fin_part, done)
                            pe.wait_ge(den_log, done)
                        else:
                            pe.wait_ge(fin, done)
                    pe.wait_ge(pl_done, it * NU + u + 1)
                    acc = ps[:, 5 + h, off:off + n]
                    v = vs[:, j, h, :]
                    pe.matmul(acc, v, ph[:, u % RP, 0:n], start=first, stop=False, skip_group_check=True)
                    last = pe.matmul(acc, v, pl[:, u % RP, 0:n], start=False, stop=end, skip_group_check=True)
                    if fox:
                        den = ps[:, 3 + h, off:off + n]
                        pe.matmul(den, c["rones"], ph[:, u % RP, 0:n], start=first, stop=False,
                                  skip_group_check=True)
                        last = pe.matmul(den, c["rones"], pl[:, u % RP, 0:n], start=False, stop=end,
                                         skip_group_check=True)
                    last.then_inc(pv_done, 1)

                def sums(u, which):
                    cc, _, h, q0, q1, _ = UNITS[u]
                    n, off = q1 - q0, q0 - QC[cc][0]
                    first = which == "ntri" and first_of_chunk(u)
                    if which == "ntri":
                        pe.wait_ge(spl_done, it * NU + u + 1)
                        if first and u >= 2:
                            pe.wait_ge(x_done, it * NU + u - 1)
                    else:
                        pe.wait_ge(x_done, it * NU + u + 1)
                    pe.matmul(ps[:, 3 + h, off:off + n], c[which], sph[:, u % 5, 0:n], start=first, stop=False,
                              skip_group_check=True)
                    pe.matmul(ps[:, 3 + h, off:off + n], c[which], spl[:, u % 5, 0:n], start=False, stop=True,
                              skip_group_check=True).then_inc(tri, 1)

                if fox:
                    pe.wait_ge(qkb, it * 2 + 2)
                    for h in range(2):
                        base = 5 * 512 * (1 - h)
                        for j in range(NBLK):
                            last = pe.matmul(psf[:, base + j * P:base + (j + 1) * P],
                                             nckp[:, h, j:j + 1].broadcast_to([P, P]), c["ident"],
                                             start=(j % 4 == 0), stop=True, skip_group_check=True)
                        last.then_inc(nck_ps, 1)
                    for h in range(2):
                        for i in range(9):
                            n = 9 * h + i
                            m = min(P, TP - i * P)
                            w = i * P + m
                            base = 5 * 512 * (n % 2)
                            if n >= 2:
                                pe.wait_ge(mxd, it * 18 + n - 1)
                            if n < 2:
                                pe.wait_ge(nck_sb, it * 2 + 2 - n)
                            q = qb[h * HD:(h + 1) * HD, i * P:(i + 1) * P]
                            for k0 in range(0, w, 512):
                                k1 = min(w, k0 + 512)
                                pe.matmul(psf[:, base + k0:base + k1], q, kb[h * HD:(h + 1) * HD, k0:k1],
                                          start=True, stop=True)
                            last = pe.matmul(psf[:, base + i * P:base + w], c["identb"],
                                             c["mask_q"][:, 0:m], start=False, stop=True,
                                             skip_group_check=True)
                            last.then_inc(s_done, 1)
                    pe.wait_ge(nm_l, it + 1)
                    for h in range(2):
                        for j in range(NBLK):
                            o = psf[:, 5 * 512 * h + j * P:5 * 512 * h + (j + 1) * P]
                            pe.matmul(o, nmh[:, h * 9 + j:h * 9 + j + 1].broadcast_to([P, P]), c["identb"],
                                      start=(j % 4 == 0), stop=False, skip_group_check=True)
                            last = pe.matmul(o, nml[:, h * 9 + j:h * 9 + j + 1].broadcast_to([P, P]),
                                             c["identb"], start=False, stop=True, skip_group_check=True)
                        last.then_inc(mr_ps, 1)
                    pe.wait_ge(mr_l, it * 2 + 2)
                    pe.wait_ge(v_lo, it * 3 + 3)
                    pe.wait_ge(dup, it * 192 + 192)
                    for s in range(NU + FL - 1):
                        if s < NU:
                            if s >= NZ:
                                pe.wait_ge(p_done, it * NU + s - NZ + 1)
                            scores(s, True)
                        if s >= FL - 1:
                            values(s - FL + 1)
                else:
                    pe.wait_ge(dup, it * 192 + 192)
                    for s in range(NU + 6):
                        if s == 3:
                            pe.wait_ge(v_nat, it * 3 + 3)
                        if s == 6:
                            pe.wait_ge(v_lo, it * 3 + 3)
                        if s < NU:
                            if s >= 3:
                                pe.wait_ge(z_kept, it * NU + s - 2)
                            scores(s, False)
                        if 5 <= s <= NU + 4 and not last_of_chunk(s - 5):
                            sums(s - 5, "nrest")
                        if 3 <= s <= NU + 2:
                            sums(s - 3, "ntri")
                        if s >= 6:
                            values(s - 6)


def decode(nc, fa, ps, psf, c, cache_k, cache_v, cache_logf, page_table, qn_d, row_d, s_d, nk_sample, nv_sample,
           nl_sample):
    NBP, NBH = NB * PAGES, NB * H_FOX
    V_SLOTS = 32
    S, s_in = fa.take(NB, PAGES, 32), fa.take(PAIRS // 2, NB * PAGES * 4)
    lfp, pt = c["lfp"], c["pt"]
    sp_ = fa.take(NB, PAGES, H_SB)
    e_ = fa.take(NB, PAGES, H_SB)
    z_ = fa.take(NB, PAGES, H_SB)
    later, laterf = fa.take(NB, PAGES, H_SB), fa.take(NB, PAGES, H_FOX)
    t_ = fa.take(NB, PAGES, H_FOX)
    rowb = fa.take(2, NB, H_FOX)
    mx, m_all, es, rs, den = (fa.take(NBH) for _ in range(5))
    mxc = fa.take(1)
    qn, kn, own = fa.take(D // 2)[0:NB, :], fa.take(D // 2)[0:NB, :], fa.take(H_FOX)[0:NB, :]
    vn = fa.take(D // 2)[0:NB, :]
    vp = fa.take(V_SLOTS, D)
    dmask, masked = fa.take(NH, HD), fa.take(2, D)
    qsel = fa.take(4)
    esn, est = fa.take(H_FOX)[0:NB, :], fa.take(NB, H_FOX)[0:NB]
    SF = S[:, :, :, H_SB:NH]
    SS = S[:, :, :, 0:H_SB]
    rows = lambda ap: ap[0].rearrange("r h d -> r (h d)")
    flat = lambda ap: ap.rearrange("p b q h -> p (b q h)")
    with ExitStack() as st:
        sem = lambda n: c["sems"](nc.semaphore(f"e_{n}"))
        v_in = [sem(f"v_in{i}") for i in range(V_SLOTS)]
        act_d, dve_d, pe_d, pool_d, load_d, v_used, own_d, own_in, scores_in, scores = (sem(n) for n in (
            "act", "dve", "pe", "pool", "load", "v_used", "own", "own_in", "scores_in", "scores"))
        block = st.enter_context(nc.Block())

        @block.sync
        def _(sp):
            sp.dma_start(s_in, s_d.rearrange("i p n -> p i n")).then_inc(scores_in, 16)
            sp.dma_start(qn, qn_d[:, D // 2:D]).then_inc(load_d, 16)
            sp.dma_start(kn, nk_sample[0, :, 0].rearrange("b h d -> b (h d)")[:, D // 2:D]).then_inc(load_d, 16)
            sp.dma_start(vn, nv_sample[0, :, 0].rearrange("b h d -> b (h d)")[:, D // 2:D]).then_inc(load_d, 16)
            sp.dma_start(rowb[:, 0], nl_sample[0, :, 0, :].partition_broadcast(P)).then_inc(load_d, 16)
            n = 0
            for bq in range(2):
                for p in range(PAGES):
                    for cc in range(4):
                        if n >= V_SLOTS:
                            sp.wait_ge(v_used, n - V_SLOTS + 1)
                        at = (4 * bq + cc) * PAGES + p
                        page = sp.value_load(pt[0:1, at:at + 1], min_val=0, max_val=cache_v.shape[1] - 1)
                        sp.dma_start(vp[:, n % V_SLOTS, :], rows(cache_v[0, bass.ds(page, 1)])
                                     ).then_inc(v_in[n % V_SLOTS], 16)
                        n += 1

        def softmax_act(act):
            act.wait_ge(scores, 9)
            act.activation(e_, SS, ACT.Exp).then_inc(act_d, 1)
            act.wait_ge(own_d, 2)
            act.dma_start(row_d[:, 0:H_FOX], own).then_inc(own_in, 16)
            act.wait_ge(own_in, 16)
            act.dma_start(rowb[:, 1], row_d[:, 0:H_FOX].partition_broadcast(P)).then_inc(own_in, 16)
            act.wait_ge(dve_d, 1)
            act.activation(e_, e_, ACT.Ln, bias=c["one"]).then_inc(act_d, 1)
            act.wait_ge(dve_d, A_X)
            act.activation(SS, z_, ACT.Exp).then_inc(act_d, 1)
            act.wait_ge(dve_d, A_S)
            act.activation(SF, t_, ACT.Exp).then_inc(act_d, 1)
            act.activation(es, es, ACT.Exp).then_inc(act_d, 1)

        steps = {}

        def dve_program(dve, dry):
            n = [0]

            def link(make):
                n[0] += 1
                if not dry:
                    make().then_inc(dve_d, 1)
                    dve.wait_ge(dve_d, n[0])

            def wait(s, v):
                if not dry:
                    dve.wait_ge(s, v)

            wait(act_d, 1)
            link(lambda: dve.tensor_scalar(e_, e_, BIG, None, ALU.min))
            if not dry:
                dve.wait_ge(load_d, 64)
                dve.tensor_tensor(qn, qn, kn, ALU.mult).then_inc(own_d, 1)
                dve.wait_ge(own_d, 1)
                dve.tensor_reduce(own, qn.rearrange("p (h d) -> p h d", d=HD), AX.X, ALU.add
                                  ).then_inc(own_d, 1)
            wait(act_d, 2)
            link(lambda: dve.tensor_tensor(sp_, e_, SS, ALU.max))
            steps["softplus"] = n[0]
            wait(pe_d, 2)
            tot = ps[:, 1, :].rearrange("p (b q h) -> p b q h", b=NB, q=PAGES)
            inner = ps[:, 0, :].rearrange("p (b q h) -> p b q h", b=NB, q=PAGES)
            link(lambda: dve.memset(later, 0.0))
            for p in range(PAGES - 2, -1, -1):
                link(lambda: dve.tensor_tensor(later[:, :, p], later[:, :, p + 1], tot[:, :, p + 1], ALU.add))
            link(lambda: dve.tensor_tensor(z_, SS, inner, ALU.add))
            link(lambda: dve.tensor_tensor(z_, z_, later, ALU.subtract))
            steps["x"] = n[0]
            wait(pe_d, 4)
            totf = ps[:, 3, :].rearrange("p (b q h) -> p b q h", b=NB, q=PAGES)
            innerf = ps[:, 2, :].rearrange("p (b q h) -> p b q h", b=NB, q=PAGES)
            link(lambda: dve.scalar_tensor_tensor(flat(t_), flat(innerf), -1.0, flat(lfp), ALU.mult,
                                                  ALU.subtract))
            link(lambda: dve.tensor_copy(laterf[:, :, PAGES - 1], rowb[:, 0]))
            for p in range(PAGES - 2, -1, -1):
                link(lambda: dve.tensor_tensor(laterf[:, :, p], laterf[:, :, p + 1], totf[:, :, p + 1],
                                               ALU.add))
            link(lambda: dve.tensor_tensor(t_, t_, laterf, ALU.add))
            link(lambda: dve.tensor_tensor(t_, t_, SF, ALU.add))
            link(lambda: dve.tensor_reduce(mx.rearrange("p (b h) -> p b h", b=NB),
                                           t_.rearrange("p b q h -> p b h q"), AX.X, ALU.max))
            steps["mx"] = n[0]
            wait(pe_d, 5)
            link(lambda: dve.tensor_reduce(mxc[0:NBH, :], ps[0:NBH, 4, 0:P], AX.X, ALU.max))
            steps["mxc"] = n[0]
            wait(pe_d, 6)
            wait(own_in, 32)
            ownb = rowb[:, 1].rearrange("p b h -> p (b h)")
            link(lambda: dve.tensor_tensor(m_all, ps[:, 5, 0:NBH], ownb, ALU.max))
            link(lambda: dve.tensor_tensor(es, ownb, m_all, ALU.subtract))
            mb = m_all.rearrange("p (b h) -> p b h", b=NB)
            for p in range(PAGES):
                link(lambda: dve.tensor_tensor(t_[:, :, p], t_[:, :, p], mb, ALU.subtract))
            steps["s"] = n[0]
            wait(act_d, 5)
            link(lambda: dve.tensor_reduce(rs.rearrange("p (b h) -> p b h", b=NB),
                                           SF.rearrange("p b q h -> p b h q"), AX.X, ALU.add))
            steps["rs"] = n[0]
            wait(pe_d, 7)
            link(lambda: dve.tensor_tensor(den, ps[:, 6, 0:NBH], es, ALU.add))
            link(lambda: dve.reciprocal(den, den))
            db = den.rearrange("p (b h) -> p b h", b=NB)
            for p in range(PAGES):
                link(lambda: dve.tensor_tensor(SF[:, :, p], SF[:, :, p], db, ALU.mult))
            link(lambda: dve.tensor_tensor(es, es, den, ALU.mult))
            steps["probs"] = n[0]
            for b in range(NB):
                link(lambda: dve.tensor_scalar(est[:, b], es[0:NB, b * H_FOX:(b + 1) * H_FOX],
                                               c["ident"][0:NB, b:b + 1], None, ALU.mult))
            link(lambda: dve.tensor_reduce(esn, est.rearrange("p b h -> p h b"), AX.X, ALU.add))
            for h in range(H_FOX):
                link(lambda: dve.tensor_scalar(vn[:, h * HD:(h + 1) * HD], vn[:, h * HD:(h + 1) * HD],
                                               esn[:, h:h + 1], None, ALU.mult))
            steps["own"] = n[0]
            wait(pool_d, 10)
            dm = dmask.rearrange("p h d -> p (h d)")
            for bq in range(2):
                wait(pe_d, 8 + bq)
                for half in range(2):
                    link(lambda: dve.tensor_tensor(masked[:, bq, half * 512:(half + 1) * 512],
                                                   ps[:, 4 + 2 * bq + half, :],
                                                   dm[:, half * 512:(half + 1) * 512], ALU.mult))
                steps[f"masked{bq}"] = n[0]
            wait(pe_d, 10)
            link(lambda: dve.tensor_copy(c["o_sample"].rearrange("p k b -> p (k b)"), ps[:, 0, 0:KT * NB]))

        dve_program(None, True)
        A_X, A_S = steps["x"], steps["s"]

        @block.scalar
        def _(act):
            softmax_act(act)

        @block.vector
        def _(dve):
            dve.memset(S[:, :, :, NH:32], 0.0).then_inc(scores, 1)
            dve.wait_ge(scores_in, 16)
            heads = S[:, :, :, 0:NH].rearrange("p b q (g i h) -> p (b q) g i h", g=2, i=PAIRS // 2)
            for i in range(PAIRS // 2):
                for g in range(2):
                    dve.tensor_copy(heads[:, :, g, i, :], s_in[:, i].rearrange(
                        "p (m g h) -> p m g h", g=2, h=2)[:, :, g, :]).then_inc(scores, 1)
            dve.wait_ge(scores, 9)
            dve_program(dve, False)

        @block.gpsimd
        def _(pool):
            pool.memset(dmask, 1.0).then_inc(pool_d, 1)
            pool.memset(qsel, 0.0).then_inc(pool_d, 1)
            pool.wait_ge(pool_d, 2)
            for cc in range(4):
                part = dmask[32 * cc:32 * cc + 32]
                pool.affine_select(out=part, in_=part, compare_op=ALU.is_equal, fill=0.0, base=0,
                                   pattern=[[-1, NH], [0, HD]], channel_multiplier=1).then_inc(pool_d, 1)
                pool.memset(qsel[32 * cc:32 * cc + 32, cc:cc + 1], 1.0).then_inc(pool_d, 1)

        @block.tensor
        def _(pe):
            def wait(name):
                pe.wait_ge(dve_d, steps[name])

            wait("softplus")
            pe.matmul(ps[:, 0, :], f(c["ntri"]), flat(sp_), start=True, stop=True).then_inc(pe_d, 1)
            pe.matmul(ps[:, 1, :], c["ones"], flat(sp_), start=True, stop=True).then_inc(pe_d, 1)
            pe.matmul(ps[:, 2, :], f(c["ntri"]), flat(lfp), start=True, stop=True).then_inc(pe_d, 1)
            pe.matmul(ps[:, 3, :], c["ones"], flat(lfp), start=True, stop=True).then_inc(pe_d, 1)
            wait("mx")
            pe.transpose(ps[0:NBH, 4, 0:P], mx, c["ident"]).then_inc(pe_d, 1)
            wait("mxc")
            pe.matmul(ps[:, 5, 0:NBH], mxc[0:NBH, :].broadcast_to([NBH, P]), c["ident"][0:NBH, 0:NBH],
                      start=True, stop=True).then_inc(pe_d, 1)
            wait("rs")
            pe.matmul(ps[:, 6, 0:NBH], c["ones"], rs, start=True, stop=True).then_inc(pe_d, 1)
            wait("probs")
            n = 0
            for bq in range(2):
                for p in range(PAGES):
                    for cc in range(4):
                        pe.wait_ge(v_in[n % V_SLOTS], 16 * (n // V_SLOTS + 1))
                        for half in range(2):
                            last = pe.matmul(ps[32 * cc:32 * cc + 32, 4 + 2 * bq + half, :],
                                             S[:, 4 * bq + cc, p, :], vp[:, n % V_SLOTS, half * 512:(half + 1) * 512],
                                             start=(p == 0), stop=(p == PAGES - 1), skip_group_check=True)
                        last.then_inc(v_used, 1)
                        n += 1
                pe.matmul(ps[:, 1, bq:bq + 1], c["ones"], c["ones"][:, 0:1], start=True, stop=True
                          ).then_inc(pe_d, 1)
            wait("masked1")
            for ft in range(KT):
                for bq in range(2):
                    o = ps[:, 0, ft * NB + 4 * bq:ft * NB + 4 * bq + 4]
                    first = ft == 0 and bq == 0
                    last = pe.matmul(o, masked[:, bq, ft * P:(ft + 1) * P], qsel, start=first, stop=ft < 4,
                                     skip_group_check=True)
                    if ft >= 4:
                        last = pe.matmul(o, vn[:, (ft - 4) * P:(ft - 3) * P],
                                         c["ident"][0:NB, 4 * bq:4 * bq + 4], start=False, stop=True,
                                         skip_group_check=True)
            last.then_inc(pe_d, 1)


def reload(nc, c, xT, oT, xT_d, oT_d):
    done = c["sems"](nc.semaphore("reloaded"))
    with nc.Block() as block:
        @block.sync
        def _(sp):
            sp.dma_start(oT[:, :, 0:TP], oT_d.rearrange("k p t -> p k t")).then_inc(done, 16)
            sp.dma_start(xT, xT_d.rearrange("k p t -> p k t")).then_inc(done, 16)
            sp.wait_ge(done, 32)

        @block.vector
        def _(dve):
            dve.tensor_copy(oT[:, :, TP:T], c["o_sample"])


def out_projection(nc, fa, ra, ps, c, hT, xT, w_out):
    raw, whi, wlo = fa.take(4, KT, P), ra.take(2, KT, P), ra.take(2, KT, P)
    N = KT // 4
    with ExitStack() as st:
        sem = lambda n: c["sems"](nc.semaphore(f"wo_{n}"))
        loaded = [sem(f"loaded{i}") for i in range(4)]
        w_hi, w_lo, proj, added = sem("hi"), sem("lo"), sem("proj"), sem("added")
        block = st.enter_context(nc.Block())

        @block.sync
        def _(sp):
            for t in range(KT):
                if t >= 4:
                    sp.wait_ge(w_lo, t - 3)
                sp.dma_start(raw[:, t % 4], w_out[0][:, t * P:(t + 1) * P].rearrange("(k p) n -> p k n", p=P)
                             ).then_inc(loaded[t % 4], 16)

        @block.scalar
        def _(act):
            for t in range(KT):
                act.wait_ge(loaded[t % 4], 16 * (t // 4 + 1))
                if t >= 2:
                    act.wait_ge(proj, 3 * (t - 1))
                act.activation(whi[:, t % 2], raw[:, t % 4], ACT.Copy).then_inc(w_hi, 1)

        @block.vector
        def _(dve):
            def add(t):
                for ci, (t0, t1) in enumerate(CH):
                    dve.wait_ge(proj, 3 * t + ci + 1)
                    dve.tensor_tensor(xT[:, t, t0:t1], xT[:, t, t0:t1], ps[:, 3 * (t % 2) + ci, 0:t1 - t0],
                                      ALU.add).then_inc(added, 1)
            for t in range(KT):
                dve.wait_ge(w_hi, t + 1)
                dve.tensor_tensor(wlo[:, t % 2], raw[:, t % 4], f(whi[:, t % 2]), ALU.subtract
                                  ).then_inc(w_lo, 1)
                if t:
                    add(t - 1)
            add(KT - 1)

        @block.tensor
        def _(pe):
            for t in range(KT):
                pe.wait_ge(w_lo, t + 1)
                for ci, (t0, t1) in enumerate(CH):
                    if t >= 2:
                        pe.wait_ge(added, 3 * (t - 2) + ci + 1)
                    product(pe, ps[:, 3 * (t % 2) + ci, 0:t1 - t0], whi[:, t % 2], wlo[:, t % 2], hT, t0, t1, KT
                            ).then_inc(proj, 1)


def mlp(nc, fa, ra, ps, c, hT, xT, w_up, w_down):
    G = 4
    JOBS = 2 * G
    N_GROUPS = FF // (G * P)
    raw, whi, wlo = fa.take(4, KT * P), ra.take(4, KT * P), ra.take(4, KT * P)
    t_, s_ = fa.take(T), fa.take(T)
    u = [ra.take(G, T), ra.take(G, T)]
    ENDS = [3 * (j + 1) for j in range(G)] + [3 * G + 6 * (j + 1) for j in range(G)]
    PER = ENDS[-1]
    CREDIT = PER - ENDS[G] + 1
    done_by = lambda it, j: it * PER + CREDIT + (ENDS[j] if j >= 0 else ENDS[j + JOBS] - PER)
    with ExitStack() as st:
        sem = lambda n: c["sems"](nc.semaphore(f"mlp_{n}"))
        loaded = [sem(f"loaded{i}") for i in range(4)]
        w_hi, w_lo, done = sem("w_hi"), sem("w_lo"), sem("done")
        relu_d, sq_d, u_hi, u_lo, down_added = (sem(n) for n in ("relu", "sq", "u_hi", "u_lo", "down_added"))
        block = st.enter_context(nc.Block())

        @block.sync
        def _(sp):
            with sp.Fori(0, N_GROUPS) as it:
                for j in range(JOBS):
                    sp.wait_ge(w_lo, it * JOBS + j + 1)
                    if j < G:
                        src = w_up[0][:, bass.ds(it * (G * P) + j * P, P)].rearrange("(k p) n -> p k n", p=P)
                        dst = raw[:, j % 4].rearrange("p (k n) -> p k n", n=P)
                    else:
                        src = w_down[0][bass.ds(it * (G * P), G * P), (j - G) * 256:(j - G + 1) * 256
                                        ].rearrange("(k p) n -> p k n", p=P)
                        dst = raw[:, j % 4].rearrange("p (k n) -> p k n", n=256)
                    sp.dma_start(dst, src).then_inc(loaded[j % 4], 16)

        @block.scalar
        def _(act):
            def weights_hi(it, j):
                act.wait_ge(loaded[j % 4], it * 32 + 16 * (j // 4 + 1))
                act.wait_ge(done, done_by(it, j - 4))
                act.activation(whi[:, j % 4], raw[:, j % 4], ACT.Copy).then_inc(w_hi, 1)

            def group(it, last):
                for j in range(JOBS):
                    if j < G:
                        if j:
                            act.wait_ge(sq_d, it * G + j)
                            act.wait_ge(u_hi, it * G + j)
                        for ci, (t0, t1) in enumerate(CH):
                            act.wait_ge(done, done_by(it, j - 1) + ci + 1)
                            act.activation(t_[:, t0:t1], ps[:, 3 * (j % 2) + ci, 0:t1 - t0], ACT.Relu
                                           ).then_inc(relu_d, 1)
                        act.wait_ge(relu_d, it * 3 * G + 3 * j + 3)
                        act.activation(u[0][:, j, :], t_, ACT.Square).then_inc(u_hi, 1)
                    if not last or j + 2 < JOBS:
                        weights_hi(it, j + 2)

            weights_hi(0, 0)
            weights_hi(0, 1)
            with act.Fori(0, N_GROUPS - 1) as it:
                group(it, False)
            group(N_GROUPS - 1, True)

        @block.vector
        def _(dve):
            def weights_lo(it, j):
                dve.wait_ge(w_hi, it * JOBS + j + 1)
                dve.tensor_tensor(wlo[:, j % 4], raw[:, j % 4], f(whi[:, j % 4]), ALU.subtract
                                  ).then_inc(w_lo, 1)

            def group(it, last):
                for j in range(JOBS):
                    if j < G:
                        dve.wait_ge(relu_d, it * 3 * G + 3 * j + 3)
                        if j:
                            dve.wait_ge(u_lo, it * G + j)
                        dve.tensor_tensor(s_, t_, t_, ALU.mult).then_inc(sq_d, 1)
                        dve.wait_ge(sq_d, it * G + j + 1)
                        dve.wait_ge(u_hi, it * G + j + 1)
                        dve.tensor_tensor(u[1][:, j, :], s_, f(u[0][:, j, :]), ALU.subtract).then_inc(u_lo, 1)
                    if not last or j + 2 < JOBS:
                        weights_lo(it, j + 2)
                    for o in range(2 * (j - G), 2 * (j - G) + 2) if j >= G else ():
                        for ci, (t0, t1) in enumerate(CH):
                            dve.wait_ge(done, done_by(it, G - 1) + 3 * o + ci + 1)
                            dve.tensor_tensor(xT[:, o, t0:t1], xT[:, o, t0:t1],
                                              ps[:, 3 * (o % 2) + ci, 0:t1 - t0], ALU.add
                                              ).then_inc(down_added, 1)

            dve.sem_inc(w_lo, 4)
            dve.sem_inc(down_added, 6)
            weights_lo(0, 0)
            weights_lo(0, 1)
            with dve.Fori(0, N_GROUPS - 1) as it:
                group(it, False)
            group(N_GROUPS - 1, True)

        @block.tensor
        def _(pe):
            pe.sem_inc(done, CREDIT)
            with pe.Fori(0, N_GROUPS) as it:
                for j in range(G):
                    w = [x[:, j % 4].rearrange("p (k n) -> p k n", n=P) for x in (whi, wlo)]
                    pe.wait_ge(w_lo, it * JOBS + 4 + j + 1)
                    for ci, (t0, t1) in enumerate(CH):
                        if j < 2:
                            pe.wait_ge(down_added, it * 3 * KT + 3 * j + ci + 1)
                        else:
                            pe.wait_ge(relu_d, it * 3 * G + 3 * (j - 2) + ci + 1)
                        product(pe, ps[:, 3 * (j % 2) + ci, 0:t1 - t0], w[0], w[1], hT, t0, t1, KT
                                ).then_inc(done, 1)
                for o in range(KT):
                    j = G + o // 2
                    n0 = (o % 2) * P
                    w = [x[:, j % 4].rearrange("p (k n) -> p k n", n=2 * P)[:, :, n0:n0 + P] for x in (whi, wlo)]
                    pe.wait_ge(w_lo, it * JOBS + 4 + j + 1)
                    for k in range(G):
                        if o == 0:
                            pe.wait_ge(u_lo, it * G + k + 1)
                        for ci, (t0, t1) in enumerate(CH):
                            if k == 0:
                                if o < 2:
                                    pe.wait_ge(relu_d, it * 3 * G + 3 * (G - 2 + o) + ci + 1)
                                else:
                                    pe.wait_ge(down_added, it * 3 * KT + 6 + 3 * (o - 2) + ci + 1)
                            out = ps[:, 3 * (o % 2) + ci, 0:t1 - t0]
                            pe.matmul(out, w[0][:, k, :], u[0][:, k, t0:t1], start=(k == 0), stop=False)
                            pe.matmul(out, w[0][:, k, :], u[1][:, k, t0:t1], start=False, stop=False)
                            last = pe.matmul(out, w[1][:, k, :], u[0][:, k, t0:t1], start=False,
                                             stop=(k == G - 1))
                            if k == G - 1:
                                last.then_inc(done, 1)


def transpose_and_store(nc, fa, ps, c, xT, y_prompt, y_sample):
    nat = fa.take(4, D)
    with ExitStack() as st:
        sem = lambda n: c["sems"](nc.semaphore(f"y_{n}"))
        stored = [sem(f"stored{i}") for i in range(4)]
        turned, moved_a, moved_v = sem("turned"), sem("moved_a"), sem("moved_v")
        block = st.enter_context(nc.Block())

        @block.sync
        def _(sp):
            for i in range(NBLK):
                sp.wait_ge(moved_a, i + 1)
                sp.wait_ge(moved_v, i + 1)
                s = nat[:, i % 4, :]
                yp = y_prompt[0]
                if i == 0:
                    sp.dma_start(yp[0:P - META, :], s[META:P, :]).then_inc(stored[0], 16)
                elif i < NBLK - 1:
                    sp.dma_start(yp[i * P - META:(i + 1) * P - META, :], s).then_inc(stored[i % 4], 16)
                else:
                    sp.dma_start(yp[SEQ - META:SEQ, :], s[0:META, :]).then_inc(stored[0], 16)
                    sp.dma_start(y_sample[:, 0, :], s[META:META + NB, :]).then_inc(stored[0], 16)
            sp.wait_ge(stored[0], 64)
            for i in range(1, 4):
                sp.wait_ge(stored[i], 32)

        @block.tensor
        def _(pe):
            for i in range(NBLK):
                m = min(P, T - i * P)
                for g in range(2):
                    if i >= 2:
                        pe.wait_ge(moved_v if g else moved_a, i - 1)
                    for k in range(4):
                        last = pe.transpose(ps[0:m, 2 * (i % 2) + g, k * P:(k + 1) * P],
                                            xT[:, 4 * g + k, i * P:i * P + m], c["ident"])
                    last.then_inc(turned, 1)

        def moves(eng, g, done, copy):
            for i in range(NBLK):
                m = min(P, T - i * P)
                eng.wait_ge(turned, 2 * i + g + 1)
                if i >= 4:
                    eng.wait_ge(stored[i % 4], 16 * (i // 4))
                copy(nat[0:m, i % 4, g * 512:(g + 1) * 512], ps[0:m, 2 * (i % 2) + g, :]).then_inc(done, 1)

        @block.scalar
        def _(act):
            moves(act, 0, moved_a, lambda o, i: act.activation(o, i, ACT.Copy))

        @block.vector
        def _(dve):
            moves(dve, 1, moved_v, dve.tensor_copy)


_INS = ["x_prompt", "x_sample", "cache_k", "cache_v", "cache_logf", "page_table", "meta_tokens", "norm_attn",
        "w_in", "b_forget", "q_norm", "k_norm", "out_norm_sb", "out_norm_fox", "w_out", "norm_mlp", "w_up",
        "w_down"]
_OUTS = [(1, SEQ, D), (NB, 1, D), (1, 1, TP, NH, HD), (1, 1, TP, NH, HD), (1, 1, TP, H_FOX),
         (1, NB, 1, NH, HD), (1, NB, 1, NH, HD), (1, NB, 1, H_FOX)]


def kernel(**inputs):
    import numpy as _np
    import concourse.bacc as _bacc
    from concourse import mybir as _mybir
    from concourse.bass_utils import run_bass_kernel_spmd as _run

    nc = _bacc.Bacc("TRN2", target_bir_lowering=False, num_devices=1)
    arrays, args = {}, []
    for name in _INS:
        a = _np.ascontiguousarray(inputs[name])
        arrays[f"in_{name}"] = a
        args.append(nc.dram_tensor(f"in_{name}", a.shape, _mybir.dt.from_np(a.dtype), kind="ExternalInput").ap())
    for i, shape in enumerate(_OUTS):
        args.append(nc.dram_tensor(f"out_{i}", shape, F32, kind="ExternalOutput").ap())
    hymba_kernel(nc, *args)
    r = _run(nc, [arrays], core_ids=[0])
    return tuple(r.results[0][f"out_{i}"] for i in range(len(_OUTS)))
```

```python
from contextlib import ExitStack

import concourse.bass as bass
import concourse.mybir as mybir
from concourse.alu_op_type import AluOpType as ALU

F32 = mybir.dt.float32
F32R = mybir.dt.float32r
BF16 = mybir.dt.bfloat16
I32 = mybir.dt.int32
ACT = mybir.ActivationFunctionType
AX = mybir.AxisListType

P = 128
D = 1024
KT = D // P
META, SEQ = 16, 1024
TP = META + SEQ
NB = 8
T = TP + NB
HD = 64
H_SB = H_FOX = 8
NH = H_SB + H_FOX
PAIRS = NH // 2
PAGES = 8
EPS = 1e-6
SCALE = HD ** -0.5
NEG = -1e30
FF = 4 * D
BIG = float(2.0 ** 60)
TW = 1152
NBLK = TW // P
CH = [(0, 350), (350, 700), (700, T)]
QC = [(0, 350), (350, 700), (700, TP)]

UNITS = []
for _c, (_a, _b) in enumerate(QC):
    for _j in range((_b - 1) // P, -1, -1):
        for _h in range(2):
            _q0 = max(_a, _j * P)
            UNITS.append((_c, _j, _h, _q0, _b, max(0, min(_b, (_j + 1) * P) - _q0)))
NU = len(UNITS)


SUM_LAG, REST_LAG = 4, 6
SUMS = []
for _s in range(NU + REST_LAG):
    if 0 <= _s - REST_LAG and UNITS[_s - REST_LAG][1]:
        SUMS.append(("nrest", _s - REST_LAG))
    if 0 <= _s - SUM_LAG < NU:
        SUMS.append(("ntri", _s - SUM_LAG))
N_SUMS = len(SUMS)


def last_of_chunk(u):
    return UNITS[u][1] == 0


def sums_through(u):
    return 1 + max(n for n, (_, v) in enumerate(SUMS) if v == u)


def first_of_chunk(u):
    c = UNITS[u][0]
    return UNITS[u][1] == (QC[c][1] - 1) // P


def finished_before(u):
    return 2 * UNITS[u][0]


class Arena:

    def __init__(self, tensor, size):
        self.t, self.size, self.at = tensor, size, 0

    def take(self, *shape, part=P):
        n = 1
        for s in shape:
            n *= s
        assert self.at + n <= self.size, (self.at, n, self.size)
        ap = self.t[0:part, self.at:self.at + n]
        self.at += n
        if len(shape) == 2:
            ap = ap.rearrange("p (a b) -> p a b", a=shape[0])
        if len(shape) == 3:
            ap = ap.rearrange("p (a b c) -> p a b c", a=shape[0], b=shape[1])
        return ap

    def back(self, at=0):
        self.at = at


def f(ap):
    return ap.bitcast(F32)


def hymba_kernel(nc, x_prompt, x_sample, cache_k, cache_v, cache_logf, page_table, meta_tokens, norm_attn,
                 w_in, b_forget, q_norm, k_norm, out_norm_sb, out_norm_fox, w_out, norm_mlp, w_up, w_down,
                 y_prompt, y_sample, nk_prompt, nv_prompt, nl_prompt, nk_sample, nv_sample, nl_sample):
    ctx = ExitStack()
    with ctx:
        xT_d = nc.dram_tensor("xT_scratch", [KT, P, T], F32).ap()
        oT_d = nc.dram_tensor("oT_scratch", [KT, P, TP], F32).ap()
        qn_d = nc.dram_tensor("q_sample_scratch", [NB, NH * HD], F32).ap()
        s_d = nc.dram_tensor("sample_scores_scratch", [PAIRS // 2, P, NB * PAGES * 4], F32).ap()
        row_d = nc.dram_tensor("row_scratch", [NB, 2 * H_FOX], F32).ap()

        def arena(stack, name, size, dtype=F32):
            return Arena(stack.enter_context(nc.sbuf_tensor(name, [P, size], dtype)), size)

        ps = ctx.enter_context(nc.psum_tensor("ps", [P, 8, 512], F32))
        psf = ps[:, :, :].rearrange("p b n -> p (b n)")
        cf, cr, cb = arena(ctx, "const_f32", 688 + NB * PAGES * (H_FOX + 1)), arena(ctx, "const_f32r", 384, F32R), arena(
            ctx, "const_bf16", 640, BF16)
        sm = cf.take(16)
        c = dict(ident=cf.take(P), ones=cf.take(P), blockones=cf.take(P), lfn=cf.take(NBLK, H_FOX),
                 nck=cf.take(H_FOX, NBLK), o_sample=cf.take(KT, NB),
                 pt=cf.take(NB * PAGES)[0:1, :].bitcast(I32), lfp=cf.take(NB, PAGES, H_FOX),
                 ntri=cr.take(P), nrest=cr.take(P), rones=cr.take(P),
                 identb=cb.take(P), mask_sb=cb.take(P), mask_fox=cb.take(P), mask_q=cb.take(P), mean=cb.take(P),
                 gain=sm[:, 0:KT], eps=sm[:, 8:9], one=sm[:, 9:10], qg=sm[:, 10:11], kg=sm[:, 11:12],
                 bf=sm[0:H_FOX, 12:13],
                 sems=None)
        held = ExitStack()
        used = []

        def hold(s):
            used.append(held.enter_context(s))
            return used[-1]

        def clear_semaphores():
            with nc.Block() as block:
                @block.sync
                def _(sp):
                    for s in used:
                        sp.sem_clear(s)
            used.clear()
            held.pop_all().close()
        c["sems"] = hold
        constants(nc, c)
        with ExitStack() as keep:
            ha = arena(keep, "h_normed", 2 * KT * T, F32R)
            hT = [ha.take(KT, T), ha.take(KT, T)]
            with ExitStack() as st:
                fa = arena(st, "load_f32", (KT + 4) * T)
                xT = fa.take(KT, T)
                kept = load_and_transpose(nc, fa, ps, c, xT, x_prompt, x_sample, meta_tokens, xT_d)
                fa.back(KT * T)
                rms(nc, "attn", fa, ps, c, xT, [(0, KT, norm_attn[0])], hT, kept=kept)
            with ExitStack() as st:
                fa, ra = arena(st, "gate_f32", 5000), arena(st, "gate_f32r", 2048, F32R)
                forget_gates(nc, fa, ra, ps, c, hT, w_in, b_forget, nl_prompt, nl_sample)
            clear_semaphores()
            with ExitStack() as st:
                fa, ra = arena(st, "pair_f32", 7704), arena(st, "pair_f32r", 15208, F32R)
                head_pairs(nc, fa, ra, ps, psf, c, hT, w_in, q_norm, k_norm, nk_prompt, nv_prompt, nk_sample,
                           nv_sample, qn_d, oT_d, s_d, cache_k, cache_logf, page_table)
        clear_semaphores()
        with ExitStack() as st:
            fa = arena(st, "decode_f32", 50000)
            decode(nc, fa, ps, psf, c, cache_k, cache_v, cache_logf, page_table, qn_d, row_d, s_d, nk_sample,
                   nv_sample, nl_sample)
        with ExitStack() as keep:
            ha = arena(keep, "h_normed2", 2 * KT * T, F32R)
            hT = [ha.take(KT, T), ha.take(KT, T)]
            xa = arena(keep, "x_f32", KT * T)
            xT = xa.take(KT, T)
            with ExitStack() as st:
                wa = arena(st, "raw_weights_f32", 4 * KT * P + T)
                raw = wa.take(4 * KT * P).rearrange("p (a k n) -> p a k n", a=4, k=KT)
                squares = wa.take(T)
                wo_in, mlp_in = ([hold(nc.semaphore(f"{n}_weights{i}")) for i in range(4)] for n in ("out", "mlp"))

                def fetch_out(sp):
                    for t in range(4):
                        out_weights(sp, w_out, raw, wo_in, t)

                def fetch_mlp(sp):
                    for j in range(4):
                        mlp_weights(sp, w_up, w_down, raw, mlp_in, 0, j)

                with ExitStack() as so:
                    fa = arena(so, "o_f32", (KT + 4) * T)
                    oT = fa.take(KT, T)
                    rms(nc, "out", fa, ps, c, oT, [(0, 4, out_norm_sb[0]), (4, 8, out_norm_fox[0])], hT,
                        loads=(oT_d, c["o_sample"], xT, xT_d), fetch=fetch_out)
                with ExitStack() as so:
                    fa, ra = arena(so, "proj_f32", 2 * T), arena(so, "proj_f32r", 4 * KT * P, F32R)
                    out_projection(nc, fa, ra, ps, c, hT, xT, w_out, raw, wo_in, squares)
                with ExitStack() as so:
                    fa = arena(so, "norm_f32", 4 * T)
                    rms(nc, "mlp", fa, ps, c, xT, [(0, KT, norm_mlp[0])], hT, fetch=fetch_mlp,
                        squares=squares)
                with ExitStack() as so:
                    fa = arena(so, "mlp_f32", 2 * T)
                    ra = arena(so, "mlp_f32r", 8 * KT * P + 8 * T, F32R)
                    mlp(nc, fa, ra, ps, c, hT, xT, w_up, w_down, raw, mlp_in)
            with ExitStack() as st:
                fa = arena(st, "store_f32", 4 * D)
                transpose_and_store(nc, fa, ps, c, xT, y_prompt, y_sample)
        held.close()


def constants(nc, c):
    with ExitStack() as st:
        stage_f = st.enter_context(nc.sbuf_tensor("stage", [P, 5, P], F32))
        built, filled = (c["sems"](nc.semaphore(n)) for n in ("built", "filled"))
        block = st.enter_context(nc.Block())
        jobs = [
            (c["ident"], 0.0, 1, -1, ALU.not_equal, 1.0),
            (stage_f[:, 0, :], -1.0, 1, -1, ALU.is_ge, 0.0),
            (stage_f[:, 1, :], -1.0, -1, 1, ALU.is_gt, 0.0),
            (stage_f[:, 2, :], 0.0, -1, 1, ALU.is_gt, NEG),
            (stage_f[:, 3, :], 0.0, -1, 1, ALU.is_ge, NEG),
            (stage_f[:, 4, :], 0.0, 1, -1, ALU.is_ge, NEG),
        ]

        @block.gpsimd
        def _(pool):
            for ap, start, _, _, _, _ in jobs:
                pool.memset(ap, start).then_inc(filled, 1)
            pool.wait_ge(filled, len(jobs))
            for ap, _, cm, step, op, fill in jobs:
                pool.affine_select(out=ap, in_=ap, compare_op=op, fill=fill, base=0, pattern=[[step, P]],
                                   channel_multiplier=cm).then_inc(built, 1)

        @block.scalar
        def _(act):
            act.preload_act_table_set("natural_log_exp_and_others")

        @block.vector
        def _(dve):
            dve.memset(c["ones"], 1.0)
            dve.memset(c["eps"], EPS)
            dve.memset(c["one"], 1.0)
            dve.memset(f(c["rones"]), 1.0)
            dve.memset(c["mean"], 1.0 / HD)
            dve.memset(c["blockones"][0:HD, 0:HD], 1.0)
            dve.memset(c["blockones"][0:HD, HD:P], 0.0)
            dve.memset(c["blockones"][HD:P, 0:HD], 0.0)
            dve.memset(c["blockones"][HD:P, HD:P], 1.0)
            dve.wait_ge(built, len(jobs))
            dve.tensor_copy(c["identb"], c["ident"])
            for n, name in enumerate(("ntri", "nrest", "mask_sb", "mask_fox", "mask_q")):
                dve.tensor_copy(c[name], stage_f[:, n, :])


def product(pe, out, whi, wlo, h, t0, t1, kt):
    for k in range(kt):
        pe.matmul(out, whi[:, k, :], h[0][:, k, t0:t1], start=(k == 0), stop=False)
        pe.matmul(out, whi[:, k, :], h[1][:, k, t0:t1], start=False, stop=False)
        last = pe.matmul(out, wlo[:, k, :], h[0][:, k, t0:t1], start=False, stop=(k == kt - 1))
    return last


def load_and_transpose(nc, fa, ps, c, xT, x_prompt, x_sample, meta_tokens, xT_d):
    nat = fa.take(4, D)
    xp = x_prompt[0]
    with ExitStack() as st:
        sem = lambda n: c["sems"](nc.semaphore(n))
        rows = [sem(f"rows{i}") for i in range(4)]
        turned, moved_a, moved_v, kept = sem("turned"), sem("moved_a"), sem("moved_v"), sem("kept")
        block = st.enter_context(nc.Block())

        @block.sync
        def _(sp):
            for i in range(NBLK):
                if i >= 4:
                    sp.wait_ge(turned, 2 * (i - 3))
                s = nat[:, i % 4, :]
                if i == 0:
                    sp.dma_start(s[0:META, :], meta_tokens).then_inc(rows[0], 16)
                    sp.dma_start(s[META:P, :], xp[0:P - META, :]).then_inc(rows[0], 16)
                elif i < NBLK - 1:
                    sp.dma_start(s, xp[i * P - META:(i + 1) * P - META, :]).then_inc(rows[i % 4], 16)
                else:
                    sp.dma_start(s[0:META, :], xp[SEQ - META:SEQ, :]).then_inc(rows[0], 16)
                    sp.dma_start(s[META:META + NB, :], x_sample[:, 0, :]).then_inc(rows[0], 16)
            sp.wait_ge(moved_a, NBLK)
            sp.wait_ge(moved_v, NBLK)
            sp.dma_start(xT_d.rearrange("k p t -> p k t"), xT).then_inc(kept, 16)

        @block.tensor
        def _(pe):
            count = [0] * 4
            for i in range(NBLK):
                count[i % 4] += 32 if i in (0, NBLK - 1) else 16
                pe.wait_ge(rows[i % 4], count[i % 4])
                m = min(P, T - i * P)
                for g in range(2):
                    if i >= 2:
                        pe.wait_ge(moved_v if g else moved_a, i - 1)
                    for k in range(4):
                        last = pe.transpose(ps[:, 2 * (i % 2) + g, k * P:k * P + m],
                                            nat[0:m, i % 4, (4 * g + k) * P:(4 * g + k + 1) * P],
                                            c["ident"][0:m, 0:m])
                    last.then_inc(turned, 1)

        def moves(eng, g, done, copy):
            for i in range(NBLK):
                m = min(P, T - i * P)
                eng.wait_ge(turned, 2 * i + g + 1)
                src = ps[:, 2 * (i % 2) + g, :].rearrange("p (k t) -> p k t", k=4)[:, :, 0:m]
                copy(xT[:, 4 * g:4 * g + 4, i * P:i * P + m], src).then_inc(done, 1)

        @block.scalar
        def _(act):
            moves(act, 0, moved_a, lambda o, i: act.activation(o, i, ACT.Copy))

        @block.vector
        def _(dve):
            moves(dve, 1, moved_v, dve.tensor_copy)
    return kept


def rms(nc, tag, fa, ps, c, xT, groups, hT, loads=None, kept=None, fetch=None, squares=None):
    at = fa.at
    sq, acc = fa.take(3, T), fa.take(T) if squares is None else squares
    ON_POOL = (1, 3, 5)
    gain = c["gain"]
    G = len(groups)
    with ExitStack() as st:
        sem = lambda n: c["sems"](nc.semaphore(f"{tag}_{n}"))
        gains, squared, added, summed, root, scaled, hi_done, lo_done, lo_pool = (sem(n) for n in (
            "gains", "squared", "added", "summed", "root", "scaled", "hi", "lo", "lo_pool"))

        def wait_lo(eng, k):
            n = len([x for x in ON_POOL if x <= k])
            eng.wait_ge(lo_done, k + 1 - n)
            if n:
                eng.wait_ge(lo_pool, n)

        if loads:
            parts, tail, other_in = [sem(f"part{i}") for i in range(G)], sem("tail"), sem("other")
        block = st.enter_context(nc.Block())

        @block.sync
        def _(sp):
            if loads:
                for part, (a, b, _) in zip(parts, groups):
                    sp.dma_start(xT[:, a:b, 0:TP], loads[0][a:b].rearrange("k p t -> p k t")).then_inc(part, 16)
            with nc.allow_non_contiguous_dma("gain columns"):
                for a, b, g in groups:
                    sp.dma_start(gain[:, a:b], g.rearrange("(k p) -> p k", p=P)).then_inc(gains, 16)
            if fetch:
                fetch(sp)
            if loads:
                sp.dma_start(loads[2], loads[3].rearrange("k p t -> p k t")).then_inc(other_in, 16)
                sp.wait_ge(other_in, 16)
            if kept is not None:
                sp.wait_ge(kept, 16)

        @block.scalar
        def _(act):
            n = 0
            if loads:
                act.wait_ge(tail, 1)
            for gi, (a, b, _) in enumerate(groups):
                if loads:
                    act.wait_ge(parts[gi], 16)
                if gi:
                    wait_lo(act, a - 1)
                for k in range(a, b) if squares is None else ():
                    if n >= 2:
                        act.wait_ge(added, n - 1)
                    act.activation(sq[:, n % 2, :], xT[:, k, :], ACT.Square).then_inc(squared, 1)
                    n += 1
                for ci, (t0, t1) in enumerate(CH):
                    act.wait_ge(summed, 3 * gi + ci + 1)
                    act.activation(acc[:, t0:t1], ps[:, ci, 0:t1 - t0], ACT.Ln,
                                   scale=1.0 / ((b - a) * P), bias=c["eps"]).then_inc(root, 1)
                act.wait_ge(root, 4 * gi + 3)
                act.activation(acc, acc, ACT.Exp, scale=-0.5).then_inc(root, 1)
                for k in range(a, b):
                    act.wait_ge(scaled, k + 1)
                    act.activation(hT[0][:, k, :], sq[:, k % 3, :], ACT.Copy).then_inc(hi_done, 1)

        @block.tensor
        def _(pe):
            n = 0
            for gi, (a, b, _) in enumerate(groups):
                n += b - a
                if squares is None:
                    pe.wait_ge(added, n)
                for ci, (t0, t1) in enumerate(CH):
                    if gi:
                        pe.wait_ge(root, 4 * gi)
                    pe.matmul(ps[:, ci, 0:t1 - t0], c["ones"], acc[:, t0:t1], start=True,
                              stop=True).then_inc(summed, 1)

        @block.vector
        def _(dve):
            n = 0
            if loads:
                dve.tensor_copy(xT[:, :, TP:T], loads[1]).then_inc(tail, 1)
                dve.wait_ge(tail, 1)
            for gi, (a, b, _) in enumerate(groups):
                for k in range(a, b) if squares is None else ():
                    dve.wait_ge(squared, n + 1)
                    if k == a:
                        dve.tensor_copy(acc, sq[:, n % 2, :]).then_inc(added, 1)
                    else:
                        dve.wait_ge(added, n)
                        dve.tensor_tensor(acc, acc, sq[:, n % 2, :], ALU.add).then_inc(added, 1)
                    n += 1
                if loads:
                    dve.wait_ge(parts[gi], 16)
                dve.wait_ge(gains, 16 * G)
                dve.wait_ge(root, 4 * gi + 4)
                def lo(k):
                    if k not in ON_POOL:
                        dve.wait_ge(hi_done, k + 1)
                        dve.tensor_tensor(hT[1][:, k, :], sq[:, k % 3, :], f(hT[0][:, k, :]), ALU.subtract
                                          ).then_inc(lo_done, 1)

                for k in range(a, b):
                    if k - a >= 3:
                        wait_lo(dve, k - 3)
                    dve.scalar_tensor_tensor(sq[:, k % 3, :], xT[:, k, :], gain[:, k:k + 1], acc, ALU.mult,
                                             ALU.mult).then_inc(scaled, 1)
                    if k > a:
                        lo(k - 1)
                lo(b - 1)
                if gi + 1 < G:
                    wait_lo(dve, b - 1)

        @block.gpsimd
        def _(pool):
            for k in ON_POOL:
                pool.wait_ge(hi_done, k + 1)
                pool.tensor_tensor(hT[1][:, k, :], sq[:, k % 3, :], f(hT[0][:, k, :]), ALU.subtract
                                   ).then_inc(lo_pool, 1)
    fa.back(at)


def forget_gates(nc, fa, ra, ps, c, hT, w_in, b_forget, nl_prompt, nl_sample):
    raw = fa.take(KT, P)
    whi, wlo = ra.take(KT, P), ra.take(KT, P)
    fb, e, lf = (fa.take(TW)[0:H_FOX, :] for _ in range(3))
    carry, lfn, nck = fa.take(H_FOX), c["lfn"], c["nck"]
    NF = H_FOX
    with ExitStack() as st:
        sem = lambda n: c["sems"](nc.semaphore(f"fg_{n}"))
        zeroed, loaded, whi_s, wlo_s, proj, biased, expd, capped, logd, gate, turned, nat, sums, stored, scan = (
            sem(n) for n in ("zeroed", "loaded", "whi", "wlo", "proj", "biased", "expd", "capped", "logd",
                             "gate", "turned", "nat", "sums", "stored", "scan"))
        block = st.enter_context(nc.Block())

        @block.sync
        def _(sp):
            sp.wait_ge(zeroed, 2)
            with nc.allow_non_contiguous_dma("eight gate columns"):
                sp.dma_start(raw[:, :, 0:NF], w_in[0][:, 6 * 512:6 * 512 + NF].rearrange(
                    "(k p) n -> p k n", p=P)).then_inc(loaded, 16)
                sp.dma_start(c["bf"], b_forget[0].rearrange("(h a) -> h a", a=1)).then_inc(loaded, 16)
                sp.wait_ge(nat, 1)
                nl = nl_prompt[0, 0]
                sp.dma_start(nl[0:D, :].rearrange("(j p) h -> p j h", p=P), lfn[:, 0:8, :]).then_inc(stored, 16)
                sp.dma_start(nl[D:TP, :], lfn[0:META, 8, :]).then_inc(stored, 16)
                sp.dma_start(nl_sample[0, :, 0, :], lfn[META:META + NB, 8, :]).then_inc(stored, 16)
                sp.wait_ge(stored, 48)

        @block.scalar
        def _(act):
            act.wait_ge(loaded, 32)
            act.activation(whi, raw, ACT.Copy).then_inc(whi_s, 1)
            for ci, (t0, t1) in enumerate(CH):
                act.wait_ge(proj, ci + 1)
                act.activation(fb[:, t0:t1], ps[0:NF, ci, 0:t1 - t0], ACT.Identity,
                               bias=c["bf"]).then_inc(biased, 1)
            act.wait_ge(biased, 3)
            act.activation(e[:, 0:T], fb[:, 0:T], ACT.Exp, scale=-1.0).then_inc(expd, 1)
            act.wait_ge(capped, 1)
            act.activation(e[:, 0:T], e[:, 0:T], ACT.Ln, bias=c["one"][0:NF, :]).then_inc(logd, 1)

        @block.tensor
        def _(pe):
            pe.wait_ge(wlo_s, 1)
            for ci, (t0, t1) in enumerate(CH):
                for k in range(KT):
                    for w, h in ((whi, hT[0]), (whi, hT[1]), (wlo, hT[0])):
                        last = pe.matmul(ps[:, ci, 0:t1 - t0], w[:, k, :], h[:, k, t0:t1],
                                         start=(k == 0 and w is whi and h is hT[0]),
                                         stop=(k == KT - 1 and w is wlo))
                last.then_inc(proj, 1)
            pe.wait_ge(gate, 1)
            for j in range(NBLK):
                last = pe.transpose(ps[:, 3, j * NF:(j + 1) * NF], lf[:, j * P:(j + 1) * P],
                                    c["ident"][0:NF, 0:NF])
            last.then_inc(turned, 1)
            pe.wait_ge(nat, 1)
            flat = lfn.rearrange("p j h -> p (j h)")
            pe.matmul(ps[:, 4, 0:NBLK * NF], f(c["nrest"]), flat, start=True, stop=True)
            pe.matmul(ps[:, 5, 0:NBLK * NF], c["ones"], flat, start=True, stop=True).then_inc(sums, 1)

        @block.vector
        def _(dve):
            dve.memset(raw, 0.0).then_inc(zeroed, 1)
            dve.memset(lf, 0.0).then_inc(zeroed, 1)
            dve.memset(carry, 0.0).then_inc(scan, 1)
            dve.wait_ge(whi_s, 1)
            dve.tensor_tensor(wlo, raw, f(whi), ALU.subtract).then_inc(wlo_s, 1)
            dve.wait_ge(expd, 1)
            dve.tensor_scalar(e[:, 0:T], e[:, 0:T], BIG, None, ALU.min).then_inc(capped, 1)
            dve.wait_ge(logd, 1)
            dve.scalar_tensor_tensor(lf[:, 0:T], e[:, 0:T], -1.0, fb[:, 0:T], ALU.mult,
                                     ALU.min).then_inc(gate, 1)
            dve.wait_ge(turned, 1)
            dve.tensor_copy(lfn, ps[:, 3, 0:NBLK * NF].rearrange("p (j h) -> p j h", h=NF)).then_inc(nat, 1)
            dve.wait_ge(sums, 1)
            dve.wait_ge(nat, 1)
            strict = ps[:, 4, 0:NBLK * NF].rearrange("p (j h) -> p h j", h=NF)
            dve.scalar_tensor_tensor(nck, lfn.rearrange("p j h -> p h j"), -1.0, strict, ALU.mult,
                                     ALU.add).then_inc(scan, 1)
            n = 2
            for j in range(NBLK):
                dve.wait_ge(scan, n)
                dve.tensor_tensor(nck[:, :, j], nck[:, :, j], carry, ALU.subtract).then_inc(scan, 1)
                dve.tensor_tensor(carry, carry, ps[:, 5, j * NF:(j + 1) * NF], ALU.add).then_inc(scan, 1)
                n += 2


def head_pairs(nc, fa, ra, ps, psf, c, hT, w_in, q_norm, k_norm, nk_prompt, nv_prompt, nk_sample, nv_sample,
               qn_d, oT_d, s_d, cache_k, cache_logf, page_table):
    nat = fa.take(2, TW)
    kn, vn = (nat[:, g].rearrange("p (a n) -> p a n", n=P) for g in range(2))
    b = dict(
        qT=fa.take(T), kT=fa.take(TW), vT=fa.take(TW), raw=fa.take(2, KT, P), nat=nat, kn=kn, vn=vn,
        qh=ra.take(2, T), ql=ra.take(2, T), ks=ra.take(2, TW), vs=ra.take(NBLK, 2, P),
        whi=ra.take(2, KT, P), wlo=ra.take(2, KT, P), hi=ra.take(TW), lo=ra.take(TW))
    with nc.Block() as block:
        @block.vector
        def _(dve):
            dve.memset(b["kT"], 0.0)
            dve.memset(b["vT"], 0.0)
    for fox in range(2):
        with ExitStack() as st:
            size_f, size_r = (8472 + 2 * KT * P - 2096, 2800) if fox else (14 * 350, 18 * 350)
            fa = Arena(st.enter_context(nc.sbuf_tensor(f"heads{fox}_f32", [P, size_f], F32)), size_f)
            ra = Arena(st.enter_context(nc.sbuf_tensor(f"heads{fox}_f32r", [P, size_r], F32R)), size_r)
            pair_loop(nc, fox, fa, ra, ps, psf, c, b, hT, w_in, q_norm, k_norm, nk_prompt, nv_prompt,
                      nk_sample, nv_sample, qn_d, oT_d, s_d, cache_k, cache_logf, page_table)


def pair_loop(nc, fox, fa, ra, ps, psf, c, b, hT, w_in, q_norm, k_norm, nk_prompt, nv_prompt, nk_sample,
              nv_sample, qn_d, oT_d, s_d, cache_k, cache_logf, page_table):
    qT, kT, vT, raw, kn, vn, qh, ql, ks, vs, whi, wlo, hi, lo = (b[n] for n in (
        "qT", "kT", "vT", "raw", "kn", "vn", "qh", "ql", "ks", "vs", "whi", "wlo", "hi", "lo"))
    dst = [qT, kT, vT]
    pt, lfp = c["pt"], c["lfp"]
    low_rows = qT
    N_IT = PAIRS // 2
    NZC, NEE, SL, RL, VL = 9, 5, SUM_LAG, REST_LAG, 8
    FL = 4
    RP = 4
    ph, pl = ra.take(RP, 350), ra.take(RP, 350)
    Z = [0, 1, 2, 7] if fox else [0, 1, 2]
    NZ = len(Z)
    if fox:
        rs = fa.take(T)
        prob = fa.take(5, 350)
        dec_s = fa.take(2 * NB, 16)
        dec_q = b["nat"][:, :, 0:NB * P].rearrange("p g (b n) -> p g b n", b=NB)
        dec_k = [t.rearrange("p (q g n) -> p q g n", q=PAGES // 2, g=2)
                 for t in (fa.take(KT * P), fa.take(KT * P), raw[:, 1].rearrange("p k n -> p (k n)"),
                           kT[:, 0:KT * P])]
        half = lambda: fa.take(T // 2).bitcast(BF16)
        nckb = [fa.take(TP), fa.take(TP)]
        mr = [t[:, 0:TP // 2].bitcast(BF16) for t in nckb]
        qb, kb, junk = fa.take(TW // 2).bitcast(BF16), half(), rs.bitcast(BF16)
        nckp, mx = fa.take(2, NBLK), fa.take(2, NBLK)
        nmh, nml = fa.take(NBLK).bitcast(BF16), fa.take(NBLK).bitcast(BF16)
        zc, ee, sph, spl = None, None, None, None
    else:
        zc, ee, sph, spl = fa.take(NZC, 350), fa.take(NEE, 350), ra.take(5, 350), ra.take(5, 350)
    tag = "fx" if fox else "sb"
    with ExitStack() as st:
        sem = lambda n: c["sems"](nc.semaphore(f"{tag}_{n}"))
        w_loaded = [sem("w_loaded0"), sem("w_loaded1")]
        w_hi, w_lo, proj, evac, carry = sem("w_hi"), sem("w_lo"), sem("proj"), sem("evac"), sem("carry")
        split_hi, split_lo, dup = sem("split_hi"), sem("split_lo"), sem("dup")
        k_turned, v_turned, k_nat, v_nat, v_hi, v_lo, stored, o_stored = (sem(n) for n in (
            "k_turned", "v_turned", "k_nat", "v_nat", "v_hi", "v_lo", "stored", "o_stored"))
        fin_moved, fin = sem("fin_moved"), sem("fin")
        pair_free, v_free = sem("pair_free"), sem("v_free")
        z_done, p_done, ph_done, pl_done, pv_done = (sem(n) for n in (
            "z_done", "p_done", "ph_done", "pl_done", "pv_done"))
        if fox:
            g_loaded, squared, ssum, root, normed, fin_part, den_log, den_inv = (sem(n) for n in (
                "g_loaded", "squared", "ssum", "root", "normed", "fin_part", "den_log", "den_inv"))
            dq_in, dk_in, dk_mult, dk_half, dk_free, ds_stored, dstep = (sem(n) for n in (
                "dq_in", "dk_in", "dk_mult", "dk_half", "dk_free", "ds_stored", "dstep"))
            act_carry = sem("act_carry")
            dk_in = [dk_in] + [sem(f"dk_in{i}") for i in range(1, 4)]
            qkb, nck_ps, nck_sb, s_done, mxd, nm_h, nm_l, mr_ps, mr_h, mr_l, setup, stepped = (sem(n) for n in (
                "qkb", "nck_ps", "nck_sb", "s_done", "mxd", "nm_h", "nm_l", "mr_ps", "mr_h", "mr_l", "setup", "stepped"))
        else:
            pt_in, lf_in, stepped = sem("pt_in"), sem("lf_in"), sem("stepped")
            e_done, z_kept, e_cap, l_done, sp_done, sph_done, spl_done, tri, x_done = (sem(n) for n in (
                "e_done", "z_kept", "e_cap", "l_done", "sp_done", "sph_done", "spl_done", "tri", "x_done"))
        block = st.enter_context(nc.Block())

        def key_page(eng, carried, it, b_, slot, m):
            page = eng.value_load(pt[0:1, bass.ds(b_ * (2 * PAGES) + slot * (PAGES // 2) + m, 1)])
            page = nc.s_assert_within(
                page, 0, cache_k.shape[1] - 1, skip_runtime_bounds_check_because=
                "the stick-breaking loop checked every entry when it loaded the gates")
            if m == 0:
                eng.wait_ge(dk_free, it * (2 * NB) + b_ * 4 + slot + 1)
                eng.sem_inc(carried, 1)
            src = cache_k[0, bass.ds(page, 1)].rearrange("a r h d -> r (a h d)").rearrange(
                "r (g n) -> r g n", g=2)[:, :, bass.ds(it * P, P)]
            eng.dma_start(dec_k[slot][:, m], src).then_inc(dk_in[slot], 16)

        @block.sync
        def _(sp):
            def load_weights(it, t):
                src = w_in[0][:, bass.ds(it * P + (fox * 3 + t) * 512, P)]
                sp.dma_start(raw[:, t % 2, :, :], src.rearrange("(k p) n -> p k n", p=P)
                             ).then_inc(w_loaded[t % 2], 16)

            load_weights(0, 0)
            load_weights(0, 1)
            if fox:
                with nc.allow_non_contiguous_dma("gain columns"):
                    for g, src in ((c["qg"], q_norm), (c["kg"], k_norm)):
                        for h in range(2):
                            sp.dma_start(g[h * HD:(h + 1) * HD, :], src[0].rearrange("(d a) -> d a", a=1)
                                         ).then_inc(g_loaded, 16)
            else:
                sp.dma_start(pt, page_table.rearrange("(a b) n -> a (b n)", a=1)).then_inc(pt_in, 16)
                sp.wait_ge(pt_in, 16)
            sp.sem_inc(pair_free, 1)
            sp.sem_inc(v_free, 1)

            def key_pages(it, b_, slots):
                for slot in slots:
                    for m in range(PAGES // 2):
                        key_page(sp, carry, it, b_, slot, m)

            with sp.Fori(0, N_IT) as it:
                sp.wait_ge(w_lo, it * 3 + 1)
                sp.sem_inc(carry, 1)
                load_weights(it, 2)
                if fox:
                    key_pages(it, 0, (0, 1))
                    sp.wait_ge(w_lo, it * 3 + 2)
                    sp.sem_inc(carry, 1)
                sp.wait_ge(split_lo, it * 2 + 1)
                for src, to in ((hi, qh), (lo, ql)):
                    for h in range(2):
                        for half_ in range(2):
                            sp.dma_start(f(to[half_ * HD:(half_ + 1) * HD, h, :]),
                                         f(src[h * HD:(h + 1) * HD, 0:T])).then_inc(dup, 16)
                sp.wait_ge(split_lo, it * 2 + 2)
                for h in range(2):
                    for n, src in enumerate((hi, lo)):
                        sp.dma_start(f(ks[n * HD:(n + 1) * HD, h, :]), f(src[h * HD:(h + 1) * HD, :])
                                     ).then_inc(dup, 16)
                if fox:
                    key_pages(it, 0, (2,))
                col = bass.ds(it * P + fox * 512, P)
                for nat, done, per, prompt, sample in ((kn, k_nat, 3, nk_prompt, nk_sample),
                                                       (vn, v_nat, 3, nv_prompt, nv_sample)):
                    sp.wait_ge(done, it * per + per)
                    sp.sem_inc(carry, 1)
                    rows = prompt[0, 0].rearrange("t h d -> t (h d)")[:, col]
                    sp.dma_start(rows[0:D, :].rearrange("(j p) n -> p j n", p=P), nat[:, 0:8, :]
                                 ).then_inc(stored, 16)
                    sp.dma_start(rows[D:TP, :], nat[0:META, 8, :]).then_inc(stored, 16)
                    sp.dma_start(sample[0, :, 0].rearrange("b h d -> b (h d)")[:, col],
                                 nat[META:META + NB, 8, :]).then_inc(stored, 16)
                with nc.allow_non_contiguous_dma("eight columns"):
                    sp.dma_start(qn_d[:, col].rearrange("b n -> n b"), qT[:, TP:T]).then_inc(stored, 16)
                sp.wait_ge(w_lo, it * 3 + 3)
                sp.sem_inc(carry, 1)
                load_weights(it + 1, 0)
                if not fox:
                    load_weights(it + 1, 1)
                if fox:
                    sp.wait_ge(v_lo, it * 3 + 3)
                    sp.sem_inc(carry, 1)
                    sp.wait_ge(stored, it * 112 + 112)
                    sp.sem_inc(carry, 1)
                    for g in range(2):
                        sp.dma_start(dec_q[:, g], qn_d[:, bass.ds(it * P + g * 512, P)].partition_broadcast(P)
                                     ).then_inc(dq_in, 16)
                    sp.wait_ge(qkb, it * 2 + 2)
                    sp.sem_inc(carry, 1)
                    key_pages(it, 0, (3,))
                    with sp.Fori(1, NB // 2) as b_:
                        key_pages(it, b_, range(3))
                    sp.wait_ge(dk_free, it * (2 * NB) + 2 * NB + 4)
                    sp.sem_inc(carry, 1)
                    sp.dma_start(s_d[bass.ds(it, 1)].rearrange("a p n -> p (a n)"),
                                 dec_s.rearrange("p b n -> p (b n)")).then_inc(ds_stored, 16)
                if not fox:
                    for m in range(2 * PAGES):
                        page = sp.value_load(pt[0:1, bass.ds(it * (2 * PAGES) + m, 1)], min_val=0,
                                             max_val=cache_k.shape[1] - 1)
                        sp.dma_start(lfp[:, bass.ds(it * 2 + m // PAGES, 1), m % PAGES, :].rearrange(
                            "p a h -> p (a h)"), cache_logf[0, bass.ds(page, 1)].rearrange("a r h -> r (a h)")
                        ).then_inc(lf_in, 16)
                    sp.wait_ge(lf_in, it * (32 * PAGES) + 32 * PAGES)
                    sp.sem_inc(stepped, 1)
                if fox:
                    load_weights(it + 1, 1)
                sp.wait_ge(fin, it * 6 + 6)
                sp.sem_inc(carry, 1)
                if not fox:
                    sp.wait_ge(stored, it * 112 + 112)
                sp.sem_inc(pair_free, 1)
                sp.dma_start(oT_d[bass.ds(it + fox * N_IT, 1)].rearrange("a p t -> p (a t)"), vT[:, 0:TP]
                             ).then_inc(o_stored, 16)
                if fox:
                    sp.wait_ge(ds_stored, it * 16 + 16)
                    sp.sem_inc(carry, 1)
                sp.wait_ge(o_stored, it * 16 + 16)
                sp.sem_inc(v_free, 1)
            for t in range(2):
                sp.wait_ge(w_loaded[t], 16 * (N_IT * (2 - t) + 1))

        @block.scalar
        def _(act):
            def weights_hi(it, t):
                act.wait_ge(w_loaded[t % 2], (it * 32 + 16 + (16 if t == 2 else 0)) if t % 2 == 0
                            else it * 16 + 16)
                if t == 2:
                    act.wait_ge(proj, it * 9 + 3)
                act.activation(whi[:, t % 2], raw[:, t % 2], ACT.Copy).then_inc(w_hi, 1)

            weights_hi(0, 0)
            with act.Fori(0, N_IT) as it:
                def take(t, chunks=(0, 1, 2)):
                    if t == 2 and chunks[0] == 0:
                        act.wait_ge(v_free, it + 1)
                    for ci in chunks:
                        t0, t1 = CH[ci]
                        act.wait_ge(proj, it * 9 + 3 * t + ci + 1)
                        act.activation(dst[t][:, t0:t1], ps[:, ci, 0:t1 - t0], ACT.Copy,
                                       scale=SCALE if (t == 0 and not fox) else 1.0).then_inc(evac, 1)

                def square(t):
                    act.wait_ge(evac, it * 9 + 3 * t + 3)
                    if t:
                        act.wait_ge(normed, it * 2 + 1)
                    act.activation(rs, dst[t][:, 0:T], ACT.Square).then_inc(squared, 1)

                def norm(t):
                    for ci, (t0, t1) in enumerate(CH):
                        act.wait_ge(ssum, it * 6 + 3 * t + 3)
                        act.activation(rs[:, t0:t1], ps[:, 3 + ci, 0:t1 - t0], ACT.Ln, scale=1.0 / HD,
                                       bias=c["eps"]).then_inc(root, 1)
                    act.wait_ge(root, it * 8 + 4 * t + 3)
                    act.activation(rs, rs, ACT.Exp, scale=-0.5).then_inc(root, 1)

                def split(t):
                    if fox:
                        act.wait_ge(normed, it * 2 + t + 1)
                    else:
                        act.wait_ge(evac, it * 9 + 3 * t + 3)
                    if t:
                        act.wait_ge(dup, it * 192 + 128)
                    w = T if t == 0 else TW
                    act.activation(hi[:, 0:w], dst[t][:, 0:w], ACT.Copy).then_inc(split_hi, 1)

                def k_rows():
                    for g in range(3):
                        act.wait_ge(k_turned, it * 3 + g + 1)
                        w = 4 if g < 2 else 1
                        act.activation(kn[:, 4 * g:4 * g + w, :], ps[:, 3 + g, 0:w * P].rearrange(
                            "p (j n) -> p j n", n=P), ACT.Copy).then_inc(k_nat, 1)

                weights_hi(it, 1)
                act.wait_ge(pair_free, it + 1)
                take(0)
                weights_hi(it, 2)
                if fox:
                    square(0)
                    take(1, (0,))
                    norm(0)
                    take(1, (1,))
                    split(0)
                    take(1, (2,))
                    square(1)
                    take(2, (0,))
                    norm(1)
                    take(2, (1,))
                    split(1)
                    take(2, (2,))
                    k_rows()
                else:
                    split(0)
                    take(1)
                    split(1)
                    take(2, (0,))
                    k_rows()
                    take(2, (1, 2))
                for g in range(3):
                    w = 4 if g < 2 else 1
                    act.wait_ge(v_nat, it * 3 + g + 1)
                    act.activation(vs[:, 4 * g:4 * g + w, :, 0:HD],
                                   vn[:, 4 * g:4 * g + w, :].rearrange("p j (h d) -> p j h d", h=2),
                                   ACT.Copy).then_inc(v_hi, 1)

                def finish(u):
                    act.wait_ge(pv_done, it * NU + u + 1)
                    cc, _, h, _, _, _ = UNITS[u]
                    n = finished_before(u) + h
                    if n:
                        act.wait_ge(fin, it * 6 + n)
                    w = QC[cc][1] - QC[cc][0]
                    act.activation(low_rows[0:HD, 0:w], ps[HD:P, 5 + h, 0:w], ACT.Copy).then_inc(fin_moved, 1)
                    if fox:
                        inv = low_rows[0:HD, 400:400 + w]
                        act.activation(inv, ps[0:HD, 3 + h, 0:w], ACT.Ln).then_inc(den_log, 1)
                        act.wait_ge(den_log, it * 6 + finished_before(u) + h + 1)
                        act.activation(inv, inv, ACT.Exp, scale=-1.0).then_inc(den_inv, 1)

                if fox:
                    for h in range(2):
                        base = 5 * 512 * (1 - h)
                        act.wait_ge(nck_ps, it * 2 + h + 1)
                        act.activation(nckb[h], psf[:, base:base + TP], ACT.Copy).then_inc(nck_sb, 1)
                    act.wait_ge(mxd, it * 18 + 18)
                    act.activation(nmh[:, 0:18], mx.rearrange("p h j -> p (h j)"), ACT.Copy,
                                   scale=-1.0).then_inc(nm_h, 1)
                    for h in range(2):
                        act.wait_ge(mr_ps, it * 2 + h + 1)
                        act.activation(mr[h][:, 0:TP], psf[:, 5 * 512 * h:5 * 512 * h + TP],
                                       ACT.Copy).then_inc(mr_h, 1)
                    for s in range(NU + FL):
                        for b_, s0 in ((1, 1), (2, 15), (3, 26)):
                            if 0 <= s - s0 < PAGES // 2:
                                key_page(act, act_carry, it, b_, 3, s - s0)
                        if s < NU:
                            cc, j, h, q0, q1, _ = UNITS[s]
                            n = q1 - q0
                            act.wait_ge(z_done, it * NU + s + 1)
                            if s >= 5:
                                act.wait_ge(pl_done, it * NU + s - 4)
                            act.activation(prob[:, s % 5, 0:n], ps[:, Z[s % NZ], 0:n], ACT.Exp,
                                           bias=nckp[:, h, j:j + 1]).then_inc(p_done, 1)
                        if s == NU - 4:
                            weights_hi(it + 1, 0)
                        if s >= FL and last_of_chunk(s - FL):
                            finish(s - FL)
                else:
                    width = lambda u: UNITS[u][4] - UNITS[u][3]
                    for s in range(NU + VL + 1):
                        if 0 <= s - 5 < NU:
                            u = s - 5
                            x = zc[:, u % NZC, 0:width(u)]
                            act.wait_ge(x_done, it * NU + u + 1)
                            act.activation(x, x, ACT.Exp).then_inc(p_done, 1)
                        if 0 <= s - 3 < NU:
                            u = s - 3
                            n = width(u)
                            act.wait_ge(sp_done, it * NU + u + 1)
                            if u >= 5:
                                act.wait_ge(tri, it * N_SUMS + sums_through(u - 5))
                            act.activation(sph[:, u % 5, 0:n], ee[:, u % NEE, 0:n], ACT.Copy).then_inc(sph_done, 1)
                        if s < NU:
                            n = width(s)
                            act.wait_ge(z_kept, it * NU + s + 1)
                            if s >= NEE:
                                act.wait_ge(spl_done, it * NU + s - NEE + 1)
                            act.activation(ee[:, s % NEE, 0:n], zc[:, s % NZC, 0:n], ACT.Exp).then_inc(e_done, 1)
                        if 0 <= s - 1 < NU:
                            u = s - 1
                            e = ee[:, u % NEE, 0:width(u)]
                            act.wait_ge(e_cap, it * NU + u + 1)
                            act.activation(e, e, ACT.Ln, bias=c["one"]).then_inc(l_done, 1)
                        if s == NU + 4:
                            weights_hi(it + 1, 0)
                        if s > VL and last_of_chunk(s - VL - 1):
                            finish(s - VL - 1)

        @block.vector
        def _(dve):
            def weights_lo(it, t):
                dve.wait_ge(w_hi, it * 3 + t + 1)
                dve.tensor_tensor(wlo[:, t % 2], raw[:, t % 2], f(whi[:, t % 2]), ALU.subtract
                                  ).then_inc(w_lo, 1)

            weights_lo(0, 0)
            if fox:
                dve.memset(qb[:, T:TW], 0.0).then_inc(setup, 1)
                dve.wait_ge(g_loaded, 64)
                dve.tensor_scalar(c["qg"], c["qg"], SCALE, None, ALU.mult).then_inc(setup, 1)
                dve.wait_ge(setup, 2)
            with dve.Fori(0, N_IT) as it:

                def norm(t):
                    dve.wait_ge(root, it * 8 + 4 * t + 4)
                    dve.scalar_tensor_tensor(dst[t][:, 0:T], dst[t][:, 0:T], c["kg" if t else "qg"], rs,
                                             ALU.mult, ALU.mult).then_inc(normed, 1)

                def split(t):
                    dve.wait_ge(split_hi, it * 2 + t + 1)
                    w = T if t == 0 else TW
                    dve.tensor_tensor(lo[:, 0:w], dst[t][:, 0:w], f(hi[:, 0:w]), ALU.subtract
                                      ).then_inc(split_lo, 1)

                weights_lo(it, 1)
                weights_lo(it, 2)
                if fox:
                    dve.tensor_copy(nckp, c["nck"][:, bass.ds(it * 2, 2), :]).then_inc(setup, 1)
                    norm(0)
                split(0)
                if fox:
                    norm(1)
                split(1)
                if fox:
                    dve.wait_ge(normed, it * 2 + 2)
                    dve.tensor_copy(qb[:, 0:T], qT).then_inc(qkb, 1)
                    dve.tensor_copy(kb[:, 0:T], kT[:, 0:T]).then_inc(qkb, 1)
                for g in range(3):
                    w = 4 if g < 2 else 1
                    dve.wait_ge(v_turned, it * 3 + g + 1)
                    dve.tensor_copy(vn[:, 4 * g:4 * g + w, :], ps[:, 5 + (g + 1) % 3, (P if g == 2 else 0):
                                                                  (P if g == 2 else 0) + w * P].rearrange(
                        "p (j n) -> p j n", n=P)).then_inc(v_nat, 1)
                for g in range(3):
                    w = 4 if g < 2 else 1
                    dve.wait_ge(v_hi, it * 3 + g + 1)
                    dve.tensor_tensor(vs[:, 4 * g:4 * g + w, :, HD:P],
                                      vn[:, 4 * g:4 * g + w, :].rearrange("p j (h d) -> p j h d", h=2),
                                      f(vs[:, 4 * g:4 * g + w, :, 0:HD]), ALU.subtract).then_inc(v_lo, 1)

                def split_p(u, src):
                    n = UNITS[u][4] - UNITS[u][3]
                    dve.wait_ge(p_done, it * NU + u + 1)
                    if u >= RP:
                        dve.wait_ge(pv_done, it * NU + u - RP + 1)
                    dve.tensor_copy(ph[:, u % RP, 0:n], src).then_inc(ph_done, 1)
                    if not fox:
                        return
                    dve.wait_ge(ph_done, it * NU + u + 1)
                    dve.tensor_tensor(pl[:, u % RP, 0:n], src, f(ph[:, u % RP, 0:n]), ALU.subtract
                                      ).then_inc(pl_done, 1)

                def finish(u):
                    cc, _, h, _, _, _ = UNITS[u]
                    n = finished_before(u) + h
                    q0, q1 = QC[cc]
                    o = vT[h * HD:(h + 1) * HD, q0:q1]
                    dve.wait_ge(fin_moved, it * 6 + n + 1)
                    if not fox:
                        dve.tensor_tensor(o, ps[0:HD, 5 + h, 0:q1 - q0], low_rows[0:HD, 0:q1 - q0], ALU.add
                                          ).then_inc(fin, 1)
                    else:
                        t0, t1 = low_rows[0:HD, 0:q1 - q0], low_rows[0:HD, 400:400 + q1 - q0]
                        dve.tensor_tensor(t0, ps[0:HD, 5 + h, 0:q1 - q0], t0, ALU.add).then_inc(fin_part, 1)
                        dve.wait_ge(den_inv, it * 6 + n + 1)
                        dve.wait_ge(fin_part, it * 6 + n + 1)
                        dve.tensor_tensor(o, t0, t1, ALU.mult).then_inc(fin, 1)

                LATE_SCORES = [4 + 31 * k // 11 for k in range(2 * NB - 4)]

                def sample_scores(k):
                    dve.wait_ge(dk_half, it * (2 * NB) + k + 1)
                    if k == 0:
                        dve.wait_ge(v_free, it + 1)
                    x = dec_k[k % 4].rearrange("p q g (h d) -> p (q g h) d", h=2)[:, :, 0:HD // 2]
                    dve.tensor_reduce(dec_s[:, k, :], x, AX.X, ALU.add).then_inc(dk_free, 1)

                if fox:
                    for n in range(18):
                        if n in (14, 17):
                            sample_scores((n - 14) // 3)
                        h, i = divmod(n, 9)
                        m = min(P, TP - i * P)
                        w = i * P + m
                        base = 5 * 512 * (n % 2)
                        dve.wait_ge(s_done, it * 18 + n + 1)
                        if n < 2:
                            dve.wait_ge(nck_sb, it * 2 + 2)
                        if n:
                            dve.wait_ge(mxd, it * 18 + n)
                        dve.sem_inc(stepped, 1)
                        dve.tensor_tensor_reduce(out=junk[:, 0:w], in0=psf[:, base:base + w],
                                                 in1=nckb[h][:, 0:w], scale=1.0, scalar=NEG, op0=ALU.add,
                                                 op1=ALU.max, accum_out=mx[:, h, i:i + 1]).then_inc(mxd, 1)
                    dve.wait_ge(nm_h, it + 1)
                    dve.wait_ge(mxd, it * 18 + 18)
                    dve.scalar_tensor_tensor(nml[:, 0:18], mx.rearrange("p h j -> p (h j)"), -1.0,
                                             nmh[:, 0:18], ALU.mult, ALU.subtract).then_inc(nm_l, 1)
                    for h in range(2):
                        dve.wait_ge(mr_h, it * 2 + h + 1)
                        lo_half = mr[h][HD:P, 0:TP]
                        dve.tensor_tensor(lo_half, psf[HD:P, 5 * 512 * h:5 * 512 * h + TP], lo_half,
                                          ALU.subtract).then_inc(mr_l, 1)
                    for k in range(2, 4):
                        sample_scores(k)
                    for u in range(NU + FL):
                        if u in LATE_SCORES:
                            sample_scores(4 + LATE_SCORES.index(u))
                        if u < NU:
                            split_p(u, prob[:, u % 5, 0:UNITS[u][4] - UNITS[u][3]])
                        if u == NU - 3:
                            weights_lo(it + 1, 0)
                        if u >= FL and last_of_chunk(u - FL):
                            finish(u - FL)
                else:
                    width = lambda u: UNITS[u][4] - UNITS[u][3]
                    for s in range(NU + VL + 1):
                        if s < NU:
                            n = width(s)
                            dve.wait_ge(z_done, it * NU + s + 1)
                            if s >= NZC:
                                dve.wait_ge(pl_done, it * NU + s - NZC + 1)
                            dve.tensor_copy(zc[:, s % NZC, 0:n], ps[:, s % 3, 0:n]).then_inc(z_kept, 1)
                        if 0 <= s - 1 < NU:
                            u = s - 1
                            e = ee[:, u % NEE, 0:width(u)]
                            dve.wait_ge(e_done, it * NU + u + 1)
                            dve.tensor_scalar(e, e, BIG, None, ALU.min).then_inc(e_cap, 1)
                        if 0 <= s - 2 < NU:
                            u = s - 2
                            n = width(u)
                            e = ee[:, u % NEE, 0:n]
                            dve.wait_ge(l_done, it * NU + u + 1)
                            dve.wait_ge(z_kept, it * NU + u + 1)
                            dve.tensor_tensor(e, e, zc[:, u % NZC, 0:n], ALU.max).then_inc(sp_done, 1)
                        if 0 <= s - 6 < NU:
                            u = s - 6
                            split_p(u, zc[:, u % NZC, 0:width(u)])
                        if 0 <= s - SL < NU:
                            u = s - SL
                            cc, _, h, q0, q1, _ = UNITS[u]
                            n, off = q1 - q0, q0 - QC[cc][0]
                            x = zc[:, u % NZC, 0:n]
                            dve.wait_ge(tri, it * N_SUMS + SUMS.index(("ntri", u)) + 1)
                            dve.tensor_tensor(x, x, ps[:, 3 + h, off:off + n], ALU.add).then_inc(x_done, 1)
                        if s == NU + 5:
                            weights_lo(it + 1, 0)
                        if s > VL and last_of_chunk(s - VL - 1):
                            finish(s - VL - 1)

        if not fox:
            @block.gpsimd
            def _(pool):
                with pool.Fori(0, N_IT) as it:
                    for s in range(NU + 4):
                        if s < NU:
                            n = UNITS[s][4] - UNITS[s][3]
                            pool.wait_ge(sph_done, it * NU + s + 1)
                            pool.tensor_tensor(spl[:, s % 5, 0:n], ee[:, s % NEE, 0:n], f(sph[:, s % 5, 0:n]),
                                               ALU.subtract).then_inc(spl_done, 1)
                        if s >= 4:
                            u = s - 4
                            n = UNITS[u][4] - UNITS[u][3]
                            pool.wait_ge(ph_done, it * NU + u + 1)
                            pool.tensor_tensor(pl[:, u % RP, 0:n], zc[:, u % NZC, 0:n], f(ph[:, u % RP, 0:n]),
                                               ALU.subtract).then_inc(pl_done, 1)
        else:
            @block.gpsimd
            def _(pool):
                pool.sem_inc(dk_free, 4)
                with pool.Fori(0, N_IT) as it:
                    pool.wait_ge(dq_in, it * 32 + 32)
                    pool.sem_inc(dstep, 1)
                    with pool.Fori(0, NB // 2) as b_:
                        for slot in range(4):
                            k = dec_k[slot]
                            pool.wait_ge(dk_in[slot], it * (64 * NB // 2) + b_ * 64 + 64)
                            pool.sem_inc(dstep, 1)
                            q = dec_q[:, :, bass.ds(b_ * 2 + slot // 2, 1), :].rearrange("p g a n -> p a g n")
                            pool.tensor_tensor(k, k, q.broadcast_to([P, PAGES // 2, 2, P]), ALU.mult
                                               ).then_inc(dk_mult, 1)
                            pool.wait_ge(dk_mult, it * (2 * NB) + b_ * 4 + slot + 1)
                            x = k.rearrange("p q g (h d) -> p (q g h) d", h=2)
                            pool.tensor_tensor(x[:, :, 0:HD // 2], x[:, :, 0:HD // 2], x[:, :, HD // 2:HD],
                                               ALU.add).then_inc(dk_half, 1)
                    pool.sem_inc(dstep, 1)

        @block.tensor
        def _(pe):
            with pe.Fori(0, N_IT) as it:
                def turn_k():
                    if fox:
                        pe.wait_ge(normed, it * 2 + 2)
                    else:
                        pe.wait_ge(evac, it * 9 + 6)
                    for g in range(3):
                        for j in range(4 * g, min(NBLK, 4 * g + 4)):
                            last = pe.transpose(ps[:, 3 + g, (j % 4) * P:(j % 4 + 1) * P],
                                                kT[:, j * P:(j + 1) * P], c["ident"])
                        last.then_inc(k_turned, 1)

                for t in range(3):
                    pe.wait_ge(w_lo, it * 3 + t + 1)
                    for ci, (t0, t1) in enumerate(CH):
                        if t:
                            pe.wait_ge(evac, it * 9 + 3 * (t - 1) + ci + 1)
                        product(pe, ps[:, ci, 0:t1 - t0], whi[:, t % 2], wlo[:, t % 2], hT, t0, t1, KT
                                ).then_inc(proj, 1)
                        if fox and t and ci == 0:
                            for cs, (s0, s1) in enumerate(CH):
                                pe.wait_ge(squared, it * 2 + t)
                                pe.matmul(ps[:, 3 + cs, 0:s1 - s0], c["blockones"], rs[:, s0:s1], start=True,
                                          stop=True).then_inc(ssum, 1)
                        if not fox and t == 2 and ci == 0:
                            turn_k()
                for g in range(3):
                    if g == 1 and fox:
                        turn_k()
                    if g == 2:
                        pe.wait_ge(k_nat, it * 3 + 3)
                    pe.wait_ge(evac, it * 9 + (9 if g else 8))
                    for j in range(4 * g, min(NBLK, 4 * g + 4)):
                        n0 = P if g == 2 else (j % 4) * P
                        last = pe.transpose(ps[:, 5 + (g + 1) % 3, n0:n0 + P], vT[:, j * P:(j + 1) * P],
                                            c["ident"])
                    last.then_inc(v_turned, 1)
                if fox:
                    pe.wait_ge(v_nat, it * 3 + 3)

                def scores(s, extra):
                    cc, j, h, q0, q1, mask = UNITS[s]
                    n = q1 - q0
                    z = ps[:, Z[s % NZ], 0:n]
                    key = ks[:, h, j * P:(j + 1) * P]
                    pe.matmul(z, key, qh[:, h, q0:q1], start=True, stop=False)
                    if mask:
                        off = q0 - j * P
                        pe.matmul(z[:, 0:mask], c["identb"],
                                  c["mask_fox" if fox else "mask_sb"][:, off:off + mask], start=False,
                                  stop=False, skip_group_check=True)
                    if extra:
                        pe.matmul(z, c["mean"], mr[h][:, q0:q1], start=False, stop=False)
                    last = pe.matmul(z, key, ql[:, h, q0:q1], start=False, stop=True)
                    last.then_inc(z_done, 1)

                def values(u):
                    cc, j, h, q0, q1, _ = UNITS[u]
                    n, off = q1 - q0, q0 - QC[cc][0]
                    first, end = first_of_chunk(u), last_of_chunk(u)
                    if first and cc:
                        done = it * 6 + 2 * (cc - 1) + h + 1
                        if fox:
                            pe.wait_ge(fin_part, done)
                            pe.wait_ge(den_log, done)
                        else:
                            pe.wait_ge(fin, done)
                    pe.wait_ge(pl_done, it * NU + u + 1)
                    acc = ps[:, 5 + h, off:off + n]
                    v = vs[:, j, h, :]
                    pe.matmul(acc, v, ph[:, u % RP, 0:n], start=first, stop=False, skip_group_check=True)
                    last = pe.matmul(acc, v, pl[:, u % RP, 0:n], start=False, stop=end, skip_group_check=True)
                    if fox:
                        den = ps[:, 3 + h, off:off + n]
                        pe.matmul(den, c["rones"], ph[:, u % RP, 0:n], start=first, stop=False,
                                  skip_group_check=True)
                        last = pe.matmul(den, c["rones"], pl[:, u % RP, 0:n], start=False, stop=end,
                                         skip_group_check=True)
                    last.then_inc(pv_done, 1)

                def sums(u, which):
                    cc, _, h, q0, q1, _ = UNITS[u]
                    n, off = q1 - q0, q0 - QC[cc][0]
                    first = which == "ntri" and first_of_chunk(u)
                    if which == "ntri":
                        pe.wait_ge(spl_done, it * NU + u + 1)
                        if first and u >= 2:
                            pe.wait_ge(x_done, it * NU + u - 1)
                    else:
                        pe.wait_ge(x_done, it * NU + u + 1)
                    pe.matmul(ps[:, 3 + h, off:off + n], c[which], sph[:, u % 5, 0:n], start=first, stop=False,
                              skip_group_check=True)
                    pe.matmul(ps[:, 3 + h, off:off + n], c[which], spl[:, u % 5, 0:n], start=False, stop=True,
                              skip_group_check=True).then_inc(tri, 1)

                if fox:
                    pe.wait_ge(qkb, it * 2 + 2)
                    for h in range(2):
                        base = 5 * 512 * (1 - h)
                        for j in range(NBLK):
                            last = pe.matmul(psf[:, base + j * P:base + (j + 1) * P],
                                             nckp[:, h, j:j + 1].broadcast_to([P, P]), c["ident"],
                                             start=(j % 4 == 0), stop=True, skip_group_check=True)
                        last.then_inc(nck_ps, 1)
                    for h in range(2):
                        for i in range(9):
                            n = 9 * h + i
                            m = min(P, TP - i * P)
                            w = i * P + m
                            base = 5 * 512 * (n % 2)
                            if n >= 2:
                                pe.wait_ge(mxd, it * 18 + n - 1)
                            if n < 2:
                                pe.wait_ge(nck_sb, it * 2 + 2 - n)
                            q = qb[h * HD:(h + 1) * HD, i * P:(i + 1) * P]
                            for k0 in range(0, w, 512):
                                k1 = min(w, k0 + 512)
                                pe.matmul(psf[:, base + k0:base + k1], q, kb[h * HD:(h + 1) * HD, k0:k1],
                                          start=True, stop=True)
                            last = pe.matmul(psf[:, base + i * P:base + w], c["identb"],
                                             c["mask_q"][:, 0:m], start=False, stop=True,
                                             skip_group_check=True)
                            last.then_inc(s_done, 1)
                    pe.wait_ge(nm_l, it + 1)
                    for h in range(2):
                        for j in range(NBLK):
                            o = psf[:, 5 * 512 * h + j * P:5 * 512 * h + (j + 1) * P]
                            pe.matmul(o, nmh[:, h * 9 + j:h * 9 + j + 1].broadcast_to([P, P]), c["identb"],
                                      start=(j % 4 == 0), stop=False, skip_group_check=True)
                            last = pe.matmul(o, nml[:, h * 9 + j:h * 9 + j + 1].broadcast_to([P, P]),
                                             c["identb"], start=False, stop=True, skip_group_check=True)
                        last.then_inc(mr_ps, 1)
                    pe.wait_ge(mr_l, it * 2 + 2)
                    pe.wait_ge(v_lo, it * 3 + 3)
                    pe.wait_ge(dup, it * 192 + 192)
                    for s in range(NU + FL - 1):
                        if s < NU:
                            if s >= NZ:
                                pe.wait_ge(p_done, it * NU + s - NZ + 1)
                            scores(s, True)
                        if s >= FL - 1:
                            values(s - FL + 1)
                else:
                    pe.wait_ge(dup, it * 192 + 192)
                    for s in range(NU + VL):
                        if s < NU:
                            if s >= 3:
                                pe.wait_ge(z_kept, it * NU + s - 2)
                            scores(s, False)
                        if s == SL:
                            pe.wait_ge(v_nat, it * 3 + 3)
                        if s == VL:
                            pe.wait_ge(v_lo, it * 3 + 3)
                        if 0 <= s - RL < NU and not last_of_chunk(s - RL):
                            sums(s - RL, "nrest")
                        if 0 <= s - SL < NU:
                            sums(s - SL, "ntri")
                        if s >= VL:
                            values(s - VL)


def decode(nc, fa, ps, psf, c, cache_k, cache_v, cache_logf, page_table, qn_d, row_d, s_d, nk_sample, nv_sample,
           nl_sample):
    NBP, NBH = NB * PAGES, NB * H_FOX
    V_SLOTS = 32
    S, s_in = fa.take(NB, PAGES, 32), fa.take(PAIRS // 2, NB * PAGES * 4)
    lfp, pt = c["lfp"], c["pt"]
    sp_ = fa.take(NB, PAGES, H_SB)
    e_ = fa.take(NB, PAGES, H_SB)
    z_ = fa.take(NB, PAGES, H_SB)
    later, laterf = fa.take(NB, PAGES, H_SB), fa.take(NB, PAGES, H_FOX)
    t_ = fa.take(NB, PAGES, H_FOX)
    rowb = fa.take(2, NB, H_FOX)
    mx, m_all, es, rs, den = (fa.take(NBH) for _ in range(5))
    mxc = fa.take(1)
    qn, kn, own = fa.take(D // 2)[0:NB, :], fa.take(D // 2)[0:NB, :], fa.take(H_FOX)[0:NB, :]
    vn = fa.take(D // 2)[0:NB, :]
    vp = fa.take(V_SLOTS, D)
    dmask, masked = fa.take(NH, HD), fa.take(2, D)
    qsel = fa.take(4)
    esn, est = fa.take(H_FOX)[0:NB, :], fa.take(NB, H_FOX)[0:NB]
    SF = S[:, :, :, H_SB:NH]
    SS = S[:, :, :, 0:H_SB]
    rows = lambda ap: ap[0].rearrange("r h d -> r (h d)")
    flat = lambda ap: ap.rearrange("p b q h -> p (b q h)")
    with ExitStack() as st:
        sem = lambda n: c["sems"](nc.semaphore(f"e_{n}"))
        v_in = [sem(f"v_in{i}") for i in range(V_SLOTS)]
        act_d, dve_d, pe_d, pool_d, load_d, v_used, own_d, own_in, scores_in, scores = (sem(n) for n in (
            "act", "dve", "pe", "pool", "load", "v_used", "own", "own_in", "scores_in", "scores"))
        block = st.enter_context(nc.Block())

        @block.sync
        def _(sp):
            sp.dma_start(s_in, s_d.rearrange("i p n -> p i n")).then_inc(scores_in, 16)
            sp.dma_start(qn, qn_d[:, D // 2:D]).then_inc(load_d, 16)
            sp.dma_start(kn, nk_sample[0, :, 0].rearrange("b h d -> b (h d)")[:, D // 2:D]).then_inc(load_d, 16)
            sp.dma_start(vn, nv_sample[0, :, 0].rearrange("b h d -> b (h d)")[:, D // 2:D]).then_inc(load_d, 16)
            sp.dma_start(rowb[:, 0], nl_sample[0, :, 0, :].partition_broadcast(P)).then_inc(load_d, 16)
            n = 0
            for bq in range(2):
                for p in range(PAGES):
                    for cc in range(4):
                        if n >= V_SLOTS:
                            sp.wait_ge(v_used, n - V_SLOTS + 1)
                        at = (4 * bq + cc) * PAGES + p
                        page = sp.value_load(pt[0:1, at:at + 1], min_val=0, max_val=cache_v.shape[1] - 1)
                        sp.dma_start(vp[:, n % V_SLOTS, :], rows(cache_v[0, bass.ds(page, 1)])
                                     ).then_inc(v_in[n % V_SLOTS], 16)
                        n += 1

        def softmax_act(act):
            act.wait_ge(scores, 9)
            act.activation(e_, SS, ACT.Exp).then_inc(act_d, 1)
            act.wait_ge(own_d, 2)
            act.dma_start(row_d[:, 0:H_FOX], own).then_inc(own_in, 16)
            act.wait_ge(own_in, 16)
            act.dma_start(rowb[:, 1], row_d[:, 0:H_FOX].partition_broadcast(P)).then_inc(own_in, 16)
            act.wait_ge(dve_d, 1)
            act.activation(e_, e_, ACT.Ln, bias=c["one"]).then_inc(act_d, 1)
            act.wait_ge(dve_d, A_X)
            act.activation(SS, z_, ACT.Exp).then_inc(act_d, 1)
            act.wait_ge(dve_d, A_S)
            act.activation(SF, t_, ACT.Exp).then_inc(act_d, 1)
            act.activation(es, es, ACT.Exp).then_inc(act_d, 1)

        steps = {}

        def dve_program(dve, dry):
            n = [0]

            def link(make):
                n[0] += 1
                if not dry:
                    make().then_inc(dve_d, 1)
                    dve.wait_ge(dve_d, n[0])

            def wait(s, v):
                if not dry:
                    dve.wait_ge(s, v)

            wait(act_d, 1)
            link(lambda: dve.tensor_scalar(e_, e_, BIG, None, ALU.min))
            if not dry:
                dve.wait_ge(load_d, 64)
                dve.tensor_tensor(qn, qn, kn, ALU.mult).then_inc(own_d, 1)
                dve.wait_ge(own_d, 1)
                dve.tensor_reduce(own, qn.rearrange("p (h d) -> p h d", d=HD), AX.X, ALU.add
                                  ).then_inc(own_d, 1)
            wait(act_d, 2)
            link(lambda: dve.tensor_tensor(sp_, e_, SS, ALU.max))
            steps["softplus"] = n[0]
            wait(pe_d, 2)
            tot = ps[:, 1, :].rearrange("p (b q h) -> p b q h", b=NB, q=PAGES)
            inner = ps[:, 0, :].rearrange("p (b q h) -> p b q h", b=NB, q=PAGES)
            link(lambda: dve.memset(later, 0.0))
            for p in range(PAGES - 2, -1, -1):
                link(lambda: dve.tensor_tensor(later[:, :, p], later[:, :, p + 1], tot[:, :, p + 1], ALU.add))
            link(lambda: dve.tensor_tensor(z_, SS, inner, ALU.add))
            link(lambda: dve.tensor_tensor(z_, z_, later, ALU.subtract))
            steps["x"] = n[0]
            wait(pe_d, 4)
            totf = ps[:, 3, :].rearrange("p (b q h) -> p b q h", b=NB, q=PAGES)
            innerf = ps[:, 2, :].rearrange("p (b q h) -> p b q h", b=NB, q=PAGES)
            link(lambda: dve.scalar_tensor_tensor(flat(t_), flat(innerf), -1.0, flat(lfp), ALU.mult,
                                                  ALU.subtract))
            link(lambda: dve.tensor_copy(laterf[:, :, PAGES - 1], rowb[:, 0]))
            for p in range(PAGES - 2, -1, -1):
                link(lambda: dve.tensor_tensor(laterf[:, :, p], laterf[:, :, p + 1], totf[:, :, p + 1],
                                               ALU.add))
            link(lambda: dve.tensor_tensor(t_, t_, laterf, ALU.add))
            link(lambda: dve.tensor_tensor(t_, t_, SF, ALU.add))
            link(lambda: dve.tensor_reduce(mx.rearrange("p (b h) -> p b h", b=NB),
                                           t_.rearrange("p b q h -> p b h q"), AX.X, ALU.max))
            steps["mx"] = n[0]
            wait(pe_d, 5)
            link(lambda: dve.tensor_reduce(mxc[0:NBH, :], ps[0:NBH, 4, 0:P], AX.X, ALU.max))
            steps["mxc"] = n[0]
            wait(pe_d, 6)
            wait(own_in, 32)
            ownb = rowb[:, 1].rearrange("p b h -> p (b h)")
            link(lambda: dve.tensor_tensor(m_all, ps[:, 5, 0:NBH], ownb, ALU.max))
            link(lambda: dve.tensor_tensor(es, ownb, m_all, ALU.subtract))
            mb = m_all.rearrange("p (b h) -> p b h", b=NB)
            for p in range(PAGES):
                link(lambda: dve.tensor_tensor(t_[:, :, p], t_[:, :, p], mb, ALU.subtract))
            steps["s"] = n[0]
            wait(act_d, 5)
            link(lambda: dve.tensor_reduce(rs.rearrange("p (b h) -> p b h", b=NB),
                                           SF.rearrange("p b q h -> p b h q"), AX.X, ALU.add))
            steps["rs"] = n[0]
            wait(pe_d, 7)
            link(lambda: dve.tensor_tensor(den, ps[:, 6, 0:NBH], es, ALU.add))
            link(lambda: dve.reciprocal(den, den))
            db = den.rearrange("p (b h) -> p b h", b=NB)
            for p in range(PAGES):
                link(lambda: dve.tensor_tensor(SF[:, :, p], SF[:, :, p], db, ALU.mult))
            link(lambda: dve.tensor_tensor(es, es, den, ALU.mult))
            steps["probs"] = n[0]
            for b in range(NB):
                link(lambda: dve.tensor_scalar(est[:, b], es[0:NB, b * H_FOX:(b + 1) * H_FOX],
                                               c["ident"][0:NB, b:b + 1], None, ALU.mult))
            link(lambda: dve.tensor_reduce(esn, est.rearrange("p b h -> p h b"), AX.X, ALU.add))
            for h in range(H_FOX):
                link(lambda: dve.tensor_scalar(vn[:, h * HD:(h + 1) * HD], vn[:, h * HD:(h + 1) * HD],
                                               esn[:, h:h + 1], None, ALU.mult))
            steps["own"] = n[0]
            wait(pool_d, 10)
            dm = dmask.rearrange("p h d -> p (h d)")
            for bq in range(2):
                wait(pe_d, 8 + bq)
                for half in range(2):
                    link(lambda: dve.tensor_tensor(masked[:, bq, half * 512:(half + 1) * 512],
                                                   ps[:, 4 + 2 * bq + half, :],
                                                   dm[:, half * 512:(half + 1) * 512], ALU.mult))
                steps[f"masked{bq}"] = n[0]
            wait(pe_d, 10)
            link(lambda: dve.tensor_copy(c["o_sample"].rearrange("p k b -> p (k b)"), ps[:, 0, 0:KT * NB]))

        dve_program(None, True)
        A_X, A_S = steps["x"], steps["s"]

        @block.scalar
        def _(act):
            softmax_act(act)

        @block.vector
        def _(dve):
            dve.memset(S[:, :, :, NH:32], 0.0).then_inc(scores, 1)
            dve.wait_ge(scores_in, 16)
            heads = S[:, :, :, 0:NH].rearrange("p b q (g i h) -> p (b q) g i h", g=2, i=PAIRS // 2)
            for i in range(PAIRS // 2):
                for g in range(2):
                    dve.tensor_copy(heads[:, :, g, i, :], s_in[:, i].rearrange(
                        "p (m g h) -> p m g h", g=2, h=2)[:, :, g, :]).then_inc(scores, 1)
            dve.wait_ge(scores, 9)
            dve_program(dve, False)

        @block.gpsimd
        def _(pool):
            pool.memset(dmask, 1.0).then_inc(pool_d, 1)
            pool.memset(qsel, 0.0).then_inc(pool_d, 1)
            pool.wait_ge(pool_d, 2)
            for cc in range(4):
                part = dmask[32 * cc:32 * cc + 32]
                pool.affine_select(out=part, in_=part, compare_op=ALU.is_equal, fill=0.0, base=0,
                                   pattern=[[-1, NH], [0, HD]], channel_multiplier=1).then_inc(pool_d, 1)
                pool.memset(qsel[32 * cc:32 * cc + 32, cc:cc + 1], 1.0).then_inc(pool_d, 1)

        @block.tensor
        def _(pe):
            def wait(name):
                pe.wait_ge(dve_d, steps[name])

            wait("softplus")
            pe.matmul(ps[:, 0, :], f(c["ntri"]), flat(sp_), start=True, stop=True).then_inc(pe_d, 1)
            pe.matmul(ps[:, 1, :], c["ones"], flat(sp_), start=True, stop=True).then_inc(pe_d, 1)
            pe.matmul(ps[:, 2, :], f(c["ntri"]), flat(lfp), start=True, stop=True).then_inc(pe_d, 1)
            pe.matmul(ps[:, 3, :], c["ones"], flat(lfp), start=True, stop=True).then_inc(pe_d, 1)
            wait("mx")
            pe.transpose(ps[0:NBH, 4, 0:P], mx, c["ident"]).then_inc(pe_d, 1)
            wait("mxc")
            pe.matmul(ps[:, 5, 0:NBH], mxc[0:NBH, :].broadcast_to([NBH, P]), c["ident"][0:NBH, 0:NBH],
                      start=True, stop=True).then_inc(pe_d, 1)
            wait("rs")
            pe.matmul(ps[:, 6, 0:NBH], c["ones"], rs, start=True, stop=True).then_inc(pe_d, 1)
            def to_features(bq):
                for ft in range(KT):
                    last = pe.matmul(ps[:, 0, ft * NB + 4 * bq:ft * NB + 4 * bq + 4],
                                     masked[:, bq, ft * P:(ft + 1) * P], qsel, start=(bq == 0 and ft == 0),
                                     stop=True, skip_group_check=True)
                return last

            wait("probs")
            n = 0
            for bq in range(2):
                for p in range(PAGES):
                    for cc in range(4):
                        pe.wait_ge(v_in[n % V_SLOTS], 16 * (n // V_SLOTS + 1))
                        for half in range(2):
                            last = pe.matmul(ps[32 * cc:32 * cc + 32, 4 + 2 * bq + half, :],
                                             S[:, 4 * bq + cc, p, :], vp[:, n % V_SLOTS, half * 512:(half + 1) * 512],
                                             start=(p == 0), stop=(p == PAGES - 1), skip_group_check=True)
                        last.then_inc(v_used, 1)
                        n += 1
                    if bq == 1 and p == PAGES // 2:
                        wait("masked0")
                        to_features(0)
                        for ft in range(4, KT):
                            pe.matmul(ps[:, 0, ft * NB:(ft + 1) * NB], vn[:, (ft - 4) * P:(ft - 3) * P],
                                      c["ident"][0:NB, 0:NB], start=False, stop=True, skip_group_check=True)
                pe.matmul(ps[:, 1, bq:bq + 1], c["ones"], c["ones"][:, 0:1], start=True, stop=True
                          ).then_inc(pe_d, 1)
            wait("masked1")
            last = to_features(1)
            last.then_inc(pe_d, 1)


def out_weights(sp, w_out, raw, loaded, t):
    sp.dma_start(raw[:, t % 4], w_out[0][:, t * P:(t + 1) * P].rearrange("(k p) n -> p k n", p=P)
                 ).then_inc(loaded[t % 4], 16)


def out_projection(nc, fa, ra, ps, c, hT, xT, w_out, raw, loaded, squares):
    sq = fa.take(2, T)
    whi, wlo = ra.take(2, KT, P), ra.take(2, KT, P)
    with ExitStack() as st:
        sem = lambda n: c["sems"](nc.semaphore(f"wo_{n}"))
        w_hi, w_lo, proj, added = sem("hi"), sem("lo"), sem("proj"), sem("added")
        squared, summed = sem("squared"), sem("summed")
        block = st.enter_context(nc.Block())

        @block.sync
        def _(sp):
            for t in range(4, KT):
                sp.wait_ge(w_lo, t - 3)
                out_weights(sp, w_out, raw, loaded, t)

        @block.scalar
        def _(act):
            for t in range(KT + 2):
                if t < KT:
                    act.wait_ge(loaded[t % 4], 16 * (t // 4 + 1))
                    if t >= 2:
                        act.wait_ge(proj, 3 * (t - 1))
                    act.activation(whi[:, t % 2], raw[:, t % 4], ACT.Copy).then_inc(w_hi, 1)
                if t >= 2:
                    act.wait_ge(added, 3 * (t - 1))
                    if t >= 4:
                        act.wait_ge(summed, t - 3)
                    act.activation(sq[:, t % 2], xT[:, t - 2, :], ACT.Square).then_inc(squared, 1)

        @block.vector
        def _(dve):
            def add(t):
                for ci, (t0, t1) in enumerate(CH):
                    dve.wait_ge(proj, 3 * t + ci + 1)
                    dve.tensor_tensor(xT[:, t, t0:t1], xT[:, t, t0:t1], ps[:, 3 * (t % 2) + ci, 0:t1 - t0],
                                      ALU.add).then_inc(added, 1)
            def add_squares(t):
                dve.wait_ge(squared, t + 1)
                if t == 0:
                    dve.tensor_copy(squares, sq[:, 0]).then_inc(summed, 1)
                else:
                    dve.wait_ge(summed, t)
                    dve.tensor_tensor(squares, squares, sq[:, t % 2], ALU.add).then_inc(summed, 1)

            for t in range(KT + 2):
                if t < KT:
                    dve.wait_ge(w_hi, t + 1)
                    dve.tensor_tensor(wlo[:, t % 2], raw[:, t % 4], f(whi[:, t % 2]), ALU.subtract
                                      ).then_inc(w_lo, 1)
                if 1 <= t <= KT:
                    add(t - 1)
                if t >= 2:
                    add_squares(t - 2)

        @block.tensor
        def _(pe):
            for t in range(KT):
                pe.wait_ge(w_lo, t + 1)
                for ci, (t0, t1) in enumerate(CH):
                    if t >= 2:
                        pe.wait_ge(added, 3 * (t - 2) + ci + 1)
                    product(pe, ps[:, 3 * (t % 2) + ci, 0:t1 - t0], whi[:, t % 2], wlo[:, t % 2], hT, t0, t1, KT
                            ).then_inc(proj, 1)


MLP_GROUP = 4


def mlp_weights(sp, w_up, w_down, raw, loaded, it, j):
    G = MLP_GROUP
    if j < G:
        src = w_up[0][:, bass.ds(it * (G * P) + j * P, P)].rearrange("(k p) n -> p k n", p=P)
        dst = raw[:, j % 4]
    else:
        src = w_down[0][bass.ds(it * (G * P), G * P), (j - G) * 256:(j - G + 1) * 256
                        ].rearrange("(k p) n -> p k n", p=P)
        dst = raw[:, j % 4].rearrange("p k n -> p (k n)").rearrange("p (k n) -> p k n", n=256)
    sp.dma_start(dst, src).then_inc(loaded[j % 4], 16)


def mlp(nc, fa, ra, ps, c, hT, xT, w_up, w_down, raw3, loaded):
    G = MLP_GROUP
    JOBS = 2 * G
    N_GROUPS = FF // (G * P)
    raw = raw3.rearrange("p a k n -> p a (k n)")
    whi, wlo = ra.take(4, KT * P), ra.take(4, KT * P)
    t_, s_ = fa.take(T), fa.take(T)
    u = [ra.take(G, T), ra.take(G, T)]
    ENDS = [3 * (j + 1) for j in range(G)] + [3 * G + 6 * (j + 1) for j in range(G)]
    PER = ENDS[-1]
    CREDIT = PER - ENDS[G] + 1
    done_by = lambda it, j: it * PER + CREDIT + (ENDS[j] if j >= 0 else ENDS[j + JOBS] - PER)
    with ExitStack() as st:
        sem = lambda n: c["sems"](nc.semaphore(f"mlp_{n}"))
        w_hi, w_lo, done, carry = sem("w_hi"), sem("w_lo"), sem("done"), sem("carry")
        relu_d, sq_d, u_hi, u_lo, down_added = (sem(n) for n in ("relu", "sq", "u_hi", "u_lo", "down_added"))
        block = st.enter_context(nc.Block())

        @block.sync
        def _(sp):
            def load(it, j):
                sp.wait_ge(w_lo, it * JOBS + j - 3)
                sp.sem_inc(carry, 1)
                mlp_weights(sp, w_up, w_down, raw3, loaded, it + j // JOBS, j % JOBS)

            with sp.Fori(0, N_GROUPS - 1) as it:
                for j in range(4, JOBS + 4):
                    load(it, j)
            for j in range(4, JOBS):
                load(N_GROUPS - 1, j)

        @block.scalar
        def _(act):
            def weights_hi(it, j):
                act.wait_ge(loaded[j % 4], it * 32 + 16 * (j // 4 + 1))
                act.wait_ge(done, done_by(it, j - 4))
                act.activation(whi[:, j % 4], raw[:, j % 4], ACT.Copy).then_inc(w_hi, 1)

            def group(it, last):
                for j in range(JOBS):
                    if j < G:
                        if j:
                            act.wait_ge(sq_d, it * G + j)
                            act.wait_ge(u_hi, it * G + j)
                        for ci, (t0, t1) in enumerate(CH):
                            act.wait_ge(done, done_by(it, j - 1) + ci + 1)
                            act.activation(t_[:, t0:t1], ps[:, 3 * (j % 2) + ci, 0:t1 - t0], ACT.Relu
                                           ).then_inc(relu_d, 1)
                        act.wait_ge(relu_d, it * 3 * G + 3 * j + 3)
                        act.activation(u[0][:, j, :], t_, ACT.Square).then_inc(u_hi, 1)
                    if not last or j + 2 < JOBS:
                        weights_hi(it, j + 2)

            weights_hi(0, 0)
            weights_hi(0, 1)
            with act.Fori(0, N_GROUPS - 1) as it:
                group(it, False)
            group(N_GROUPS - 1, True)

        @block.vector
        def _(dve):
            def weights_lo(it, j):
                dve.wait_ge(w_hi, it * JOBS + j + 1)
                dve.tensor_tensor(wlo[:, j % 4], raw[:, j % 4], f(whi[:, j % 4]), ALU.subtract
                                  ).then_inc(w_lo, 1)

            def group(it, last):
                for j in range(JOBS):
                    if j < G:
                        dve.wait_ge(relu_d, it * 3 * G + 3 * j + 3)
                        if j:
                            dve.wait_ge(u_lo, it * G + j)
                        dve.tensor_tensor(s_, t_, t_, ALU.mult).then_inc(sq_d, 1)
                        dve.wait_ge(sq_d, it * G + j + 1)
                        dve.wait_ge(u_hi, it * G + j + 1)
                        dve.tensor_tensor(u[1][:, j, :], s_, f(u[0][:, j, :]), ALU.subtract).then_inc(u_lo, 1)
                    if not last or j + 2 < JOBS:
                        weights_lo(it, j + 2)
                    for o in range(2 * (j - G), 2 * (j - G) + 2) if j >= G else ():
                        for ci, (t0, t1) in enumerate(CH):
                            dve.wait_ge(done, done_by(it, G - 1) + 3 * o + ci + 1)
                            dve.tensor_tensor(xT[:, o, t0:t1], xT[:, o, t0:t1],
                                              ps[:, 3 * (o % 2) + ci, 0:t1 - t0], ALU.add
                                              ).then_inc(down_added, 1)

            dve.sem_inc(down_added, 6)
            weights_lo(0, 0)
            weights_lo(0, 1)
            with dve.Fori(0, N_GROUPS - 1) as it:
                group(it, False)
            group(N_GROUPS - 1, True)

        @block.tensor
        def _(pe):
            pe.sem_inc(done, CREDIT)
            with pe.Fori(0, N_GROUPS) as it:
                for j in range(G):
                    w = [x[:, j % 4].rearrange("p (k n) -> p k n", n=P) for x in (whi, wlo)]
                    pe.wait_ge(w_lo, it * JOBS + j + 1)
                    for ci, (t0, t1) in enumerate(CH):
                        if j < 2:
                            pe.wait_ge(down_added, it * 3 * KT + 3 * j + ci + 1)
                        else:
                            pe.wait_ge(relu_d, it * 3 * G + 3 * (j - 2) + ci + 1)
                        product(pe, ps[:, 3 * (j % 2) + ci, 0:t1 - t0], w[0], w[1], hT, t0, t1, KT
                                ).then_inc(done, 1)
                for o in range(KT):
                    j = G + o // 2
                    n0 = (o % 2) * P
                    w = [x[:, j % 4].rearrange("p (k n) -> p k n", n=2 * P)[:, :, n0:n0 + P] for x in (whi, wlo)]
                    pe.wait_ge(w_lo, it * JOBS + j + 1)
                    for k in range(G):
                        if o == 0:
                            pe.wait_ge(u_lo, it * G + k + 1)
                        for ci, (t0, t1) in enumerate(CH):
                            if k == 0:
                                if o < 2:
                                    pe.wait_ge(relu_d, it * 3 * G + 3 * (G - 2 + o) + ci + 1)
                                else:
                                    pe.wait_ge(down_added, it * 3 * KT + 6 + 3 * (o - 2) + ci + 1)
                            out = ps[:, 3 * (o % 2) + ci, 0:t1 - t0]
                            pe.matmul(out, w[0][:, k, :], u[0][:, k, t0:t1], start=(k == 0), stop=False)
                            pe.matmul(out, w[0][:, k, :], u[1][:, k, t0:t1], start=False, stop=False)
                            last = pe.matmul(out, w[1][:, k, :], u[0][:, k, t0:t1], start=False,
                                             stop=(k == G - 1))
                            if k == G - 1:
                                last.then_inc(done, 1)


def transpose_and_store(nc, fa, ps, c, xT, y_prompt, y_sample):
    nat = fa.take(4, D)
    with ExitStack() as st:
        sem = lambda n: c["sems"](nc.semaphore(f"y_{n}"))
        stored = [sem(f"stored{i}") for i in range(4)]
        turned, moved_a, moved_v = sem("turned"), sem("moved_a"), sem("moved_v")
        block = st.enter_context(nc.Block())

        @block.sync
        def _(sp):
            for i in range(NBLK):
                sp.wait_ge(moved_a, i + 1)
                sp.wait_ge(moved_v, i + 1)
                s = nat[:, i % 4, :]
                yp = y_prompt[0]
                if i == 0:
                    sp.dma_start(yp[0:P - META, :], s[META:P, :]).then_inc(stored[0], 16)
                elif i < NBLK - 1:
                    sp.dma_start(yp[i * P - META:(i + 1) * P - META, :], s).then_inc(stored[i % 4], 16)
                else:
                    sp.dma_start(yp[SEQ - META:SEQ, :], s[0:META, :]).then_inc(stored[0], 16)
                    sp.dma_start(y_sample[:, 0, :], s[META:META + NB, :]).then_inc(stored[0], 16)
            sp.wait_ge(stored[0], 64)
            for i in range(1, 4):
                sp.wait_ge(stored[i], 32)

        @block.tensor
        def _(pe):
            for i in range(NBLK):
                m = min(P, T - i * P)
                for g in range(2):
                    if i >= 2:
                        pe.wait_ge(moved_v if g else moved_a, i - 1)
                    for k in range(4):
                        last = pe.transpose(ps[0:m, 2 * (i % 2) + g, k * P:(k + 1) * P],
                                            xT[:, 4 * g + k, i * P:i * P + m], c["ident"])
                    last.then_inc(turned, 1)

        def moves(eng, g, done, copy):
            for i in range(NBLK):
                m = min(P, T - i * P)
                eng.wait_ge(turned, 2 * i + g + 1)
                if i >= 4:
                    eng.wait_ge(stored[i % 4], 16 * (i // 4))
                copy(nat[0:m, i % 4, g * 512:(g + 1) * 512], ps[0:m, 2 * (i % 2) + g, :]).then_inc(done, 1)

        @block.scalar
        def _(act):
            moves(act, 0, moved_a, lambda o, i: act.activation(o, i, ACT.Copy))

        @block.vector
        def _(dve):
            moves(dve, 1, moved_v, dve.tensor_copy)


_INS = ["x_prompt", "x_sample", "cache_k", "cache_v", "cache_logf", "page_table", "meta_tokens", "norm_attn",
        "w_in", "b_forget", "q_norm", "k_norm", "out_norm_sb", "out_norm_fox", "w_out", "norm_mlp", "w_up",
        "w_down"]
_OUTS = [(1, SEQ, D), (NB, 1, D), (1, 1, TP, NH, HD), (1, 1, TP, NH, HD), (1, 1, TP, H_FOX),
         (1, NB, 1, NH, HD), (1, NB, 1, NH, HD), (1, NB, 1, H_FOX)]


def kernel(**inputs):
    import numpy as _np
    import concourse.bacc as _bacc
    from concourse import mybir as _mybir
    from concourse.bass_utils import run_bass_kernel_spmd as _run

    nc = _bacc.Bacc("TRN2", target_bir_lowering=False, num_devices=1)
    arrays, args = {}, []
    for name in _INS:
        a = _np.ascontiguousarray(inputs[name])
        arrays[f"in_{name}"] = a
        args.append(nc.dram_tensor(f"in_{name}", a.shape, _mybir.dt.from_np(a.dtype), kind="ExternalInput").ap())
    for i, shape in enumerate(_OUTS):
        args.append(nc.dram_tensor(f"out_{i}", shape, F32, kind="ExternalOutput").ap())
    hymba_kernel(nc, *args)
    r = _run(nc, [arrays], core_ids=[0])
    return tuple(r.results[0][f"out_{i}"] for i in range(len(_OUTS)))
```
